# Optimizing a Trainium2 kernel written in Bass

```python
import math
import jax, jax.numpy as jnp
from jax import lax
import numpy as np

D_MODEL = 1024
BATCH = 1
SEQ = 512
DEPTH = 4

N_MIXERS = 3
RMS_EPS = 1e-6

DN_HEADS = 8
DN_DK = 128
DN_DV = 256
DN_QK_W = DN_HEADS * DN_DK
DN_V_W = DN_HEADS * DN_DV
DN_CONV = 4
DN_CHUNK = 64
DN_CONV_W = 2 * DN_QK_W + DN_V_W
DN_IN = DN_CONV_W + DN_V_W + 2 * DN_HEADS

SB_HEADS = 16
SB_DH = 64
SB_W = SB_HEADS * SB_DH
SB_BLOCK = 128
SB_IN = 4 * SB_W

SC_W = 2 * D_MODEL
SC_CONV = 3
SC_IN = 4 * SC_W

N_DN = (DEPTH + 2) // 3
N_SB = (DEPTH + 1) // 3
N_SC = DEPTH // 3

kernel_name = "interleaved_deltanet_stickbreak_shortconv"

def rms_norm(x, g, eps=RMS_EPS):
    xf = x.astype(jnp.float32)
    y = xf * lax.rsqrt(jnp.mean(xf * xf, axis=-1, keepdims=True) + eps)
    return (y * g.astype(jnp.float32)).astype(x.dtype)

def l2_norm(x, eps=1e-6):
    xf = x.astype(jnp.float32)
    return xf * lax.rsqrt(jnp.sum(xf * xf, axis=-1, keepdims=True) + eps)

def causal_dwconv(x, w):
    K, C = w.shape
    return lax.conv_general_dilated(
        x, w[:, None, :].astype(x.dtype), window_strides=(1,), padding=[(K - 1, 0)],
        dimension_numbers=('NWC', 'WIO', 'NWC'), feature_group_count=C)

def gated_delta_rule(q, k, v, log_a, beta):
    f32 = jnp.float32
    Bn, T, H, dk = q.shape
    dv = v.shape[-1]
    C = DN_CHUNK
    N = T // C

    def chunks(t):
        t = t.astype(f32).reshape((Bn, N, C, H) + t.shape[3:])
        return jnp.moveaxis(t, 3, 1)

    q = chunks(q) * (dk ** -0.5)
    k = chunks(k)
    v = chunks(v)
    beta = chunks(beta)
    g = jnp.cumsum(chunks(log_a), axis=-1)
    causal = jnp.tril(jnp.ones((C, C), bool))
    strict = jnp.tril(jnp.ones((C, C), bool), -1)
    gdiff = g[..., :, None] - g[..., None, :]
    decay = jnp.where(causal, jnp.exp(jnp.where(causal, gdiff, 0.0)), 0.0)

    k_beta = k * beta[..., None]
    L = jnp.where(strict, jnp.einsum('bhncd,bhnsd->bhncs', k_beta, k) * decay, 0.0)
    eye = jnp.eye(C, dtype=f32)
    rhs = jnp.concatenate([v * beta[..., None], k_beta * jnp.exp(g)[..., None]], axis=-1)
    sol = lax.linalg.triangular_solve(L + eye, rhs, left_side=True, lower=True, unit_diagonal=True)
    u, w = sol[..., :dv], sol[..., dv:]

    intra = jnp.where(causal, jnp.einsum('bhncd,bhnsd->bhncs', q, k) * decay, 0.0)
    q_dec = q * jnp.exp(g)[..., None]
    g_last = g[..., -1]
    k_dec = k * jnp.exp(g_last[..., None] - g)[..., None]

    def step(S, xs):
        q_c, k_c, u_c, w_c, a_c, gl = xs
        v_new = u_c - jnp.einsum('bhcd,bhde->bhce', w_c, S)
        o = jnp.einsum('bhcd,bhde->bhce', q_c, S) + jnp.einsum('bhcs,bhse->bhce', a_c, v_new)
        S = S * jnp.exp(gl)[..., None, None] + jnp.einsum('bhcd,bhce->bhde', k_c, v_new)
        return S, o

    xs = tuple(jnp.moveaxis(t, 2, 0) for t in (q_dec, k_dec, u, w, intra, g_last))
    S0 = jnp.zeros((Bn, H, dk, dv), f32)
    _, o = lax.scan(step, S0, xs)
    return jnp.transpose(o, (1, 0, 3, 2, 4)).reshape(Bn, T, H, dv)

def deltanet_mixer(h, w_in, conv_w, a_log, dt_bias, o_norm_g, w_out):
    f32 = jnp.float32
    Bn, T, _ = h.shape
    proj = h @ w_in
    qkv, gate, a_in, b_in = jnp.split(proj, [DN_CONV_W, DN_CONV_W + DN_V_W, DN_CONV_W + DN_V_W + DN_HEADS], axis=-1)
    qkv = jax.nn.silu(causal_dwconv(qkv, conv_w))
    q, k, v = jnp.split(qkv, [DN_QK_W, 2 * DN_QK_W], axis=-1)
    q = l2_norm(q.reshape(Bn, T, DN_HEADS, DN_DK))
    k = l2_norm(k.reshape(Bn, T, DN_HEADS, DN_DK))
    v = v.reshape(Bn, T, DN_HEADS, DN_DV)
    beta = jax.nn.sigmoid(b_in.astype(f32))
    log_a = -jnp.exp(a_log.astype(f32)) * jax.nn.softplus(a_in.astype(f32) + dt_bias.astype(f32))
    o = gated_delta_rule(q, k, v, log_a, beta)
    o = rms_norm(o, o_norm_g) * jax.nn.silu(gate.astype(f32).reshape(Bn, T, DN_HEADS, DN_DV))
    return o.reshape(Bn, T, DN_V_W).astype(h.dtype) @ w_out

def stick_breaking_mixer(h, w_in, q_norm_g, k_norm_g, w_out):
    f32 = jnp.float32
    Bn, T, _ = h.shape
    q, k, v, gate = jnp.split(h @ w_in, 4, axis=-1)
    q = rms_norm(q.reshape(Bn, T, SB_HEADS, SB_DH), q_norm_g)
    k = rms_norm(k.reshape(Bn, T, SB_HEADS, SB_DH), k_norm_g)
    v = v.reshape(Bn, T, SB_HEADS, SB_DH)
    nb = T // SB_BLOCK
    qb = jnp.moveaxis(q.reshape(Bn, nb, SB_BLOCK, SB_HEADS, SB_DH), 1, 0)
    key_pos = jnp.arange(T)
    scale = SB_DH ** -0.5

    def block(args):
        i, q_blk = args
        q_pos = i * SB_BLOCK + jnp.arange(SB_BLOCK)
        z = jnp.einsum('bqhd,bshd->bhqs', q_blk, k, preferred_element_type=f32) * scale
        mask = key_pos[None, :] < q_pos[:, None]
        log1m = jnp.where(mask, -jax.nn.softplus(z), 0.0)
        after = lax.cumsum(log1m, axis=3, reverse=True) - log1m
        wts = jnp.where(mask, jnp.exp(jax.nn.log_sigmoid(z) + after), 0.0)
        return jnp.einsum('bhqs,bshd->bqhd', wts.astype(v.dtype), v)

    o = lax.map(block, (jnp.arange(nb), qb))
    o = jnp.moveaxis(o, 0, 1).reshape(Bn, T, SB_W)
    return (o * jax.nn.silu(gate)) @ w_out

def short_conv_mixer(h, w_in, conv_w, w_out):
    b_gate, c_gate, u, gate = jnp.split(h @ w_in, 4, axis=-1)
    y = b_gate * causal_dwconv(c_gate * u, conv_w)
    return (y * jax.nn.silu(gate)) @ w_out

def setup_inputs(seed: int = 0) -> dict:
    key = jax.random.key(seed)
    ks = jax.random.split(key, 16)
    f32 = jnp.float32

    def dense(k, shape, fan_in):
        return jax.random.normal(k, shape, f32) * fan_in ** -0.5

    def gain(k, shape):
        return 1.0 + 0.05 * jax.random.normal(k, shape, f32)

    x = jax.random.normal(ks[0], (BATCH, SEQ, D_MODEL), f32)
    norm_g = gain(ks[1], (DEPTH, D_MODEL))
    dn_w_in = dense(ks[2], (N_DN, D_MODEL, DN_IN), D_MODEL)
    dn_conv_w = dense(ks[3], (N_DN, DN_CONV, DN_CONV_W), DN_CONV)
    dn_a_log = jnp.log(jax.random.uniform(ks[4], (N_DN, DN_HEADS), f32, 1.0, 16.0))
    dt = jnp.exp(jax.random.uniform(ks[5], (N_DN, DN_HEADS), f32, math.log(1e-3), math.log(1e-1)))
    dn_dt_bias = dt + jnp.log(-jnp.expm1(-dt))
    dn_o_norm_g = gain(ks[6], (N_DN, DN_DV))
    dn_w_out = dense(ks[7], (N_DN, DN_V_W, D_MODEL), DN_V_W)
    sb_w_in = dense(ks[8], (N_SB, D_MODEL, SB_IN), D_MODEL)
    sb_q_norm_g = gain(ks[9], (N_SB, SB_DH))
    sb_k_norm_g = gain(ks[10], (N_SB, SB_DH))
    sb_w_out = dense(ks[11], (N_SB, SB_W, D_MODEL), SB_W)
    sc_w_in = dense(ks[12], (N_SC, D_MODEL, SC_IN), D_MODEL)
    sc_conv_w = dense(ks[13], (N_SC, SC_CONV, SC_W), SC_CONV)
    sc_w_out = dense(ks[14], (N_SC, SC_W, D_MODEL), SC_W)
    return {"x": x, "norm_g": norm_g,
            "dn_w_in": dn_w_in, "dn_conv_w": dn_conv_w, "dn_a_log": dn_a_log, "dn_dt_bias": dn_dt_bias,
            "dn_o_norm_g": dn_o_norm_g, "dn_w_out": dn_w_out,
            "sb_w_in": sb_w_in, "sb_q_norm_g": sb_q_norm_g, "sb_k_norm_g": sb_k_norm_g, "sb_w_out": sb_w_out,
            "sc_w_in": sc_w_in, "sc_conv_w": sc_conv_w, "sc_w_out": sc_w_out}

def reference(x, norm_g, dn_w_in, dn_conv_w, dn_a_log, dn_dt_bias, dn_o_norm_g, dn_w_out,
              sb_w_in, sb_q_norm_g, sb_k_norm_g, sb_w_out, sc_w_in, sc_conv_w, sc_w_out):
    for i in range(DEPTH):
        h = rms_norm(x, norm_g[i])
        j = i // N_MIXERS
        kind = i % N_MIXERS
        if kind == 0:
            y = deltanet_mixer(h, dn_w_in[j], dn_conv_w[j], dn_a_log[j], dn_dt_bias[j], dn_o_norm_g[j], dn_w_out[j])
        elif kind == 1:
            y = stick_breaking_mixer(h, sb_w_in[j], sb_q_norm_g[j], sb_k_norm_g[j], sb_w_out[j])
        else:
            y = short_conv_mixer(h, sc_w_in[j], sc_conv_w[j], sc_w_out[j])
        x = x + y
    return x


_drawn_inputs = setup_inputs


def setup_inputs(seed=0):
    import zlib

    import numpy as np

    out = dict(_drawn_inputs(seed))
    spreads = {}
    factors = {'sb_q_norm_g': 4.993, 'sb_k_norm_g': 4.968}
    for name, (base, spread) in spreads.items():
        noise = np.random.default_rng([zlib.crc32(name.encode()), seed]).standard_normal(out[name].shape)
        drawn = base * np.exp(spread * noise) if base else spread * noise
        out[name] = __import__('jax').numpy.asarray(drawn.astype(out[name].dtype))
    for name, factor in factors.items():
        out[name] = (out[name] * factor).astype(out[name].dtype)
    return out
```

```python
from concourse import mybir
import concourse.bass as bass

F32 = mybir.dt.float32
F32R = mybir.dt.float32r
BF16 = mybir.dt.bfloat16
ALU = mybir.AluOpType
ACT = mybir.ActivationFunctionType

P = 128
T = 512
D = 1024
KD = D // P
NB = T // P
EPS = 1e-6

HEADS = 8
GR = 4
NG = HEADS // GR
LEVELS = 7
SB_PAIRS = 8

WT = 2048

DN, SB, SC = 0, 1, 2
TILES = {DN: 1 + 16 + 8 + 8, SB: 4 + 8 + 4 + 4, SC: 32 + 8}

C_ID, C_ONES, C_BLOCK, C_TRI, C_NEG, C_SELK = 0, 128, 256, 384, 512, 640
NCF = C_SELK + 64
B_ID, B_STRICT, B_INCL, B_LEVEL = 0, 128, 256, 384
B_SEL = B_LEVEL + (LEVELS - 1) * P
B_SUB = B_SEL + HEADS * P
NCB = B_SUB + P


def param_columns(layers):
    at, cols = 0, []
    for kind in layers:
        c = {"norm": at}
        at += KD
        if kind == DN:
            c |= {"conv": at, "dt": at + 128, "alog": at + 129, "onorm": at + 130}
            at += 132
        elif kind == SB:
            c |= {"q": at, "k": at + 1}
            at += 2
        else:
            c |= {"conv": at}
            at += 48
        cols.append(c)
    return cols, at


def y_at(c):
    return (c + 8) % 16


def walk(eng, first, n, step):
    step(first, 0, 0)
    step(first + 1, 0, 1)
    if n > 4:
        with eng.Fori(0, (n - 4) // 2) as i:
            step(first + 2, i, 2)
            step(first + 3, i, 3)
    step(first + n - 2, 0, n - 2)
    step(first + n - 1, 0, n - 1)


def trunk(nc, layers, x_in, tiles, params, const_f, const_b, out):
    cols, n_params = param_columns(layers)
    n_tiles = sum(TILES[k] for k in layers)
    tile_base = [sum(TILES[k] for k in layers[:l]) for l in range(len(layers))]
    nth = [layers[:l].count(k) for l, k in enumerate(layers)]

    at = [1152]

    def sb(name, shape, dt=F32, offset=None):
        size = 2 if dt == BF16 else 4
        for s in shape[1:]:
            size *= s
        if offset is None:
            offset = at[0]
            at[0] += (size + 31) // 32 * 32
        return nc.alloc_sbuf_tensor_at(name, shape, dt, offset=offset)

    x = sb("x", [P, KD, T])
    h_hi = sb("h_hi", [P, KD, T], F32R)
    h_lo = sb("h_lo", [P, KD, T], F32R)
    w_raw = sb("w_raw", [P, 2, WT])
    w_hi = sb("w_hi", [P, 2, WT], F32R)
    w_lo = sb("w_lo", [P, 2, WT], F32R)
    big_at = at[0]
    big = sb("big", [P, 32, T])
    y_hi = sb("y_hi", [P, 16, T], F32R, offset=big_at)
    y_lo = sb("y_lo", [P, 16, T], F32R, offset=big_at + 16 * T * 4)
    v_tok = sb("v_tok", [P, NB, D], offset=big_at)
    o_sb = sb("o_sb", [P, SB_PAIRS, T], offset=big_at + 24 * T * 4)

    arena = at[0]
    at[0] += 48 * 1024

    def in_arena(name, word, shape, dt=F32):
        return sb(name, shape, dt, offset=arena + 4 * word)

    cf = sb("cf", [P, NCF])
    cb = sb("cb", [P, NCB], BF16)
    par = sb("par", [P, n_params])
    rows = sb("rows", [P, T])
    row_parts = sb("row_parts", [P, 3, T], BF16)
    rows_b = sb("rows_b", [P, P])
    tok = sb("tok", [P, P])
    bexp = sb("bexp", [P, HEADS])
    g_end = sb("g_end", [P, HEADS])
    tok_neg = sb("tok_neg", [P, HEADS])
    gq8 = sb("gq8", [P, 1])
    assert at[0] <= nc.sbuf_usable_end, (at[0], nc.sbuf_usable_end)

    ident = cf[:, C_ID:C_ID + P]
    ones = cf[:, C_ONES:C_ONES + P]

    sq = in_arena("sq", 0, [P, 2, T])
    rstd = in_arena("rstd", 1024, [P, T])
    hf = in_arena("hf", 1536, [P, 2, T])
    acc = in_arena("acc", 2560, [P, 4, T])
    sp_a = in_arena("sp_a", 4608, [P, T])
    sp_b = in_arena("sp_b", 5120, [P, T])
    sp_c = in_arena("sp_c", 5632, [P, T])
    gate = in_arena("gate", 6144, [P, 4, T])
    yf = in_arena("yf", 8192, [P, 4, T])
    nsq = in_arena("nsq", 10240, [P, 3, T])
    nr = in_arena("nr", 11776, [P, T])
    mid = in_arena("mid", 8192, [P, T], BF16)
    ksq = in_arena("ksq", 6144, [P, 2, T])
    rk_ln = in_arena("rk_ln", 7168, [P, T])
    kn = in_arena("kn", 0, [P, HEADS, P])
    attn_t = in_arena("attn_t", 1024, [P, HEADS, P])
    inv_t = in_arena("inv_t", 2048, [P, HEADS, P])
    q_dec = in_arena("q_dec", 3072, [P, HEADS, P])
    decay = in_arena("decay", 4096, [P, HEADS, P])
    inv = in_arena("inv", 5120, [P, HEADS, P])
    l_t = in_arena("l_t", 6144, [P, HEADS, P])
    prod = in_arena("prod", 7168, [P, HEADS, P])
    vb = in_arena("vb", 8192, [P, HEADS, 2 * P])
    state = in_arena("state", 10240, [P, HEADS, 2 * P])
    k_beta = inv
    k_in = inv
    k_out = l_t
    w_neg = prod
    sb_sp = in_arena("sb_sp", 0, [P, 2, 1280])
    sb_w = in_arena("sb_w", 2560, [P, 2, T])
    sb_t = in_arena("sb_t", 3584, [P, 2, T])
    sb_sq = in_arena("sb_sq", 4608, [P, 2, T])
    sb_raw = in_arena("sb_raw", 5632, [P, 2, T])
    sb_r = in_arena("sb_r", 6656, [P, 2, T])
    sb_qk = in_arena("sb_qk", 7680, [P, 2, 2, T])
    sb_v = in_arena("sb_v", 9728, [P, 2, NB, P])
    sc_c = in_arena("sc_c", 2560, [P, T])
    sc_cu = in_arena("sc_cu", 3072, [P, T + 2])
    sc_acc = in_arena("sc_acc", 3600, [P, T])
    sc_y = in_arena("sc_y", 4112, [P, T])
    sc_gate = in_arena("sc_gate", 4624, [P, T])
    sc_yf = in_arena("sc_yf", 5136, [P, T])

    ps = [nc.alloc_psum_tensor(f"ps{i}", [P, T], F32) for i in range(8)]

    def bank(s, c):
        return ps[2 * (s % 2) + c]

    def sem(name):
        return nc.alloc_semaphore(name)

    loaded = sem("const_loaded")
    x_loaded = [sem(f"x_loaded{m}") for m in range(KD // 2)]
    raw = [sem("raw0_loaded"), sem("raw1_loaded")]
    hi_done, lo_done = sem("w_hi_done"), sem("w_lo_done")
    proj_done, proj_free = sem("proj_done"), sem("proj_free")
    stored = sem("stored")
    sq_done, sum_done = sem("x_sq_done"), sem("x_sum_done")
    ss_done = sem("x_ss_done")
    x_done = sem("x_done")
    ln_done, rstd_done = sem("ln_done"), sem("rstd_done")
    hf_done, hhi_done, h_done = sem("hf_done"), sem("hhi_done"), sem("h_done")
    yf_done, yhi_done, y_done = sem("yf_done"), sem("yhi_done"), sem("y_done")
    dn_a, dn_v = sem("dn_rows_act"), sem("dn_rows_dve")
    zeroed = sem("rows_zeroed")
    conv_step, conv_done, silu_done = sem("conv_step"), sem("conv_done"), sem("silu_done")
    part_step, parts_done = sem("row_part_step"), sem("row_parts_done")
    ksq_done, kss_done = sem("ksq_done"), sem("kss_done")
    names = ("rows_b gbc rkbc bbc tokt vt gmask kk qk xt pm du turned ktok wt vn ot ot0 su "
             "kn kbeta tok tokneg qdec gend bexp vb lt at u0 u0i pe_p ue xe kin kout sst "
             "vstage vstage2 gbc2 eg tokexp dec x0 wneg vne oe sz").split()
    s = {n: sem("dn_" + n) for n in names}
    PE_AHEAD, ACT_AHEAD = ("tokt", "wt", "vn", "ot", "su"), ("wneg", "vne", "oe")
    nsum_done = sem("o_sq_summed")
    nsq_done, nss_done, nln_done, nr_done, on_done, gate_done = (
        sem(n) for n in ("o_sq_done", "o_ss_done", "o_ln_done", "o_rstd_done", "o_norm_done", "gate_done"))
    b = {n: sem("sb_" + n) for n in
         "gq8 vev sq raw ss ln r qk v z abs exp ln1 sp cum w pv ev gate".split()}
    c_ = {n: sem("sc_" + n) for n in "zero c cu cstep conv y gate".split()}

    dn_gate0 = [tile_base[l] + 17 for l in range(len(layers))]
    y_base = []
    n_y = 0
    for kind in layers:
        y_base.append(n_y)
        n_y += 8 if kind == SB else 16

    block = nc.Block()
    blk = block.__enter__()

    @blk.sync
    def _(sp):
        for m in range(KD // 2):
            sp.dma_start(x[:, 2 * m:2 * m + 2, :], x_in[:, 2 * m:2 * m + 2, :]).then_inc(x_loaded[m], 16)
        sp.dma_start(cf[:, :], const_f).then_inc(loaded, 16)
        sp.dma_start(par[:, :], params).then_inc(loaded, 16)
        sp.dma_start(cb[:, :], const_b).then_inc(loaded, 16)
        for t in range(2):
            sp.dma_start(w_raw[:, t, :], tiles[t]).then_inc(raw[t], 16)
        pairs = n_tiles // 2
        with sp.Fori(1, pairs) as i:
            for t in range(2):
                sp.wait_ge(lo_done, 2 * i + t - 1)
                sp.dma_start(w_raw[:, t, :], tiles[2 * i + t]).then_inc(raw[t], 16)
        if n_tiles % 2:
            sp.wait_ge(lo_done, n_tiles - 2)
            sp.dma_start(w_raw[:, 0, :], tiles[n_tiles - 1]).then_inc(raw[0], 16)
        for m in range(KD):
            sp.wait_ge(x_done, KD * (len(layers) - 1) + m + 1)
            sp.dma_start(out[:, m, :], x[:, m, :]).then_inc(stored, 16)
        sp.wait_ge(stored, 16 * KD)

    @blk.gpsimd
    def _(pool):
        pool.memset(rows[:, :], 0.0).then_inc(zeroed, 1)
        pool.memset(row_parts[:, :, :], 0.0).then_inc(zeroed, 1)

        def low(t, i, slot):
            pool.wait_ge(hi_done, 2 * i + t + 1)
            pool.tensor_tensor(w_lo[:, slot, :], w_raw[:, slot, :], w_hi[:, slot, :].bitcast(F32),
                               ALU.subtract).then_inc(lo_done, 1)

        def lows(first, n):
            with pool.Fori(0, n // 2) as i:
                low(first, i, first % 2)
                low(first + 1, i, (first + 1) % 2)
            if n % 2:
                low(first + n - 1, 0, (first + n - 1) % 2)

        def chunks(d):
            with pool.Fori(0, NB) as bi:
                def v(per, k):
                    return NB * d * per + bi * per + k

                pool.wait_ge(s["su"], v(4, 1))
                pool.wait_ge(silu_done, 32 * (d + 1))
                pool.tensor_copy(l_t[:, :, :], big[:, 24:32, bass.ts(bi, P)]).then_inc(s["vstage2"], 1)
                for g in range(NG):
                    pool.wait_ge(s["ot"], v(4, 1))
                    pool.wait_ge(s["eg"], v(2, g + 1))
                    gs = slice(GR * g, GR * g + GR)
                    pool.tensor_tensor(q_dec[:, gs, :], decay[:, gs, :], big[:, gs, bass.ts(bi, P)], ALU.mult)\
                        .then_inc(s["qdec"], 1)

        for l, kind in enumerate(layers):
            if kind == DN:
                lows(tile_base[l], 18)
                chunks(nth[l])
                lows(tile_base[l] + 18, TILES[kind] - 18)
            else:
                lows(tile_base[l], TILES[kind])

    @blk.scalar
    def _(act):
        def settle():
            act.wait_ge(loaded, 48)

        def exp_and_ln():
            act.preload_act_table_set("natural_log_exp_and_others")

        def hi(t, i=0):
            if t >= n_tiles:
                return
            act.wait_ge(raw[t % 2], 16 * (t // 2 + 1) + 16 * i)
            if t >= 2:
                act.wait_ge(proj_done, 2 * (t - 1) + 4 * i)
            act.activation(w_hi[:, t % 2, :], w_raw[:, t % 2, :], ACT.Copy).then_inc(hi_done, 1)

        def square_x(l, m, i=0, per=1):
            n = KD * l + m + 2 * per * i
            if l:
                act.wait_ge(x_done, n - KD + 1)
            if isinstance(i, int) and m < 2:
                if l:
                    act.wait_ge(ss_done, l)
            else:
                act.wait_ge(sum_done, n - l - 1)
            settle()
            act.activation(sq[:, m % 2, :], x[:, m + 2 * per * i, :], ACT.Square).then_inc(sq_done, 1)

        def norm(l):
            exp_and_ln()
            hi(tile_base[l] + 1)
            act.wait_ge(ss_done, l + 1)
            act.activation(rstd[:, :], ps[7][:, :], ACT.Ln, scale=1.0 / D, bias=EPS).then_inc(ln_done, 1)
            act.wait_ge(ln_done, l + 1)
            act.activation(rstd[:, :], rstd[:, :], ACT.Exp, scale=-0.5).then_inc(rstd_done, 1)
            for k in range(KD):
                act.wait_ge(hf_done, KD * l + k + 1)
                act.activation(h_hi[:, k, :], hf[:, k % 2, :], ACT.Copy).then_inc(hhi_done, 1)

        def out_steps(l, first, n, per):
            more = l + 1 < len(layers)

            def step(t, i, k):
                if not (isinstance(i, int) and k == n - 1 and more):
                    hi(t + 1, i)
                if more and not (isinstance(i, int) and k == 0):
                    for c in range(per):
                        square_x(l + 1, per * (k - 1) + c, i, per)

            walk(act, first, n, step)
            if more:
                for c in range(per):
                    square_x(l + 1, per * (n - 1) + c, 0, per)
                hi(first + n)

        def deltanet(l):
            d, t0, c0 = nth[l], tile_base[l], cols[l]
            bk = bank(t0, 0)
            act.wait_ge(proj_done, 2 * (t0 + 1))
            a0 = 6 * d
            act.wait_ge(dn_v, 9 * d + 1)
            act.activation(sp_a[0:8, :], bk[0:8, :], ACT.Abs, bias=par[0:8, c0["dt"]:c0["dt"] + 1]).then_inc(dn_a, 1)
            act.wait_ge(dn_a, a0 + 1)
            act.activation(sp_a[0:8, :], sp_a[0:8, :], ACT.Exp, scale=-1.0).then_inc(dn_a, 1)
            act.wait_ge(dn_a, a0 + 2)
            act.activation(sp_a[0:8, :], sp_a[0:8, :], ACT.Ln, bias=1.0).then_inc(dn_a, 1)
            act.activation(sp_c[32:40, :], bk[32:40, :], ACT.Exp, scale=-1.0).then_inc(dn_a, 1)
            act.activation(bexp[0:8, 0:1], par[0:8, c0["alog"]:c0["alog"] + 1], ACT.Exp).then_inc(dn_a, 1)
            act.wait_ge(dn_v, 9 * d + 9)
            act.activation(rows[96:104, :], sp_b[0:8, :], ACT.Exp).then_inc(dn_a, 1)

            def silu(k, i=0):
                for c in range(2):
                    act.wait_ge(conv_done, 32 * d + 2 * k + c + 1 + 4 * i)
                    settle()
                    act.activation(big[:, 2 * k + c + 4 * i, :], acc[:, 2 * (k % 2) + c, :], ACT.Silu)\
                        .then_inc(silu_done, 1)

            def step(t, i, k):
                hi(t + 1, i)
                if not (isinstance(i, int) and k == 0):
                    silu(k - 1, i)

            walk(act, t0 + 1, 8, step)
            for k in range(8, 8 + HEADS // 2):
                step(t0 + 1 + k, 0, k)
                for h in (2 * k - 16, 2 * k - 15):
                    act.wait_ge(silu_done, 32 * d + 9 + h)
                    if h >= 2:
                        act.wait_ge(kss_done, HEADS * d + h - 1)
                    act.activation(ksq[:, h % 2, :], big[:, HEADS + h, :], ACT.Square).then_inc(ksq_done, 1)
            step(t0 + 13, 0, 12)
            exp_and_ln()
            act.wait_ge(kss_done, HEADS * (d + 1))
            act.activation(rk_ln[0:8, :], ps[7][0:8, :], ACT.Ln, bias=EPS).then_inc(s["sz"], 1)
            act.wait_ge(s["sz"], 2 * d + 1)
            act.activation(rows[64:72, :], rk_ln[0:8, :], ACT.Exp, scale=-0.5).then_inc(s["sz"], 1)
            for k in range(13, 16):
                step(t0 + 1 + k, 0, k)
            silu(15)
            exp_and_ln()
            act.wait_ge(s["sz"], 2 * d + 2)

            with act.Fori(0, NB) as bi:
                def v(per, k):
                    return NB * d * per + bi * per + k

                act.wait_ge(dn_a, a0 + 6)
                act.wait_ge(s["gend"], NB * d + d + 1 + bi)
                act.wait_ge(s["tokt"], v(1, 1))
                settle()
                act.activation(rows_b[:, :], rows[:, bass.ts(bi, P)], ACT.Copy).then_inc(s["rows_b"], 1)
                act.wait_ge(s["vn"], v(4, 1))
                act.wait_ge(silu_done, 32 * (d + 1))
                settle()
                act.activation(prod[:, :, :], big[:, 16:24, bass.ts(bi, P)], ACT.Copy).then_inc(s["vstage"], 1)
                act.wait_ge(s["ot"], v(4, 1))
                act.wait_ge(s["tokneg"], v(1, 1))
                for h in range(HEADS):
                    if h % GR == 0:
                        act.wait_ge(s["gmask"], v(2, h // GR + 1))
                    act.activation(attn_t[:, h, :], ps[h // GR][:, (h % GR) * P:(h % GR) * P + P], ACT.Exp,
                                   bias=tok_neg[:, h:h + 1]).then_inc(s["dec"], 1)
                act.wait_ge(s["tok"], v(1, 1))
                act.activation(bexp[:, :], tok[:, 0:8], ACT.Exp).then_inc(s["tokexp"], 1)
                for g in range(NG):
                    act.wait_ge(s["xt"], v(2, g + 1))
                    act.activation(inv[:, GR * g:GR * g + GR, :], ps[g][:, :], ACT.Copy).then_inc(s["x0"], 1)
                act.wait_ge(s["sst"], NB * d * 8 + 8 * d + 8 + bi * 8)
                for g in range(NG):
                    act.wait_ge(s["gbc2"], v(2, g + 1))
                    act.activation(decay[:, GR * g:GR * g + GR, :], ps[4 + g][:, :], ACT.Exp).then_inc(s["eg"], 1)
                n_l = LEVELS - 1
                for lv in range(n_l - 1):
                    for g in range(NG):
                        act.wait_ge(s["turned"], v(2 * (n_l - 1), 2 * lv + g + 1))
                        act.activation(inv[:, GR * g:GR * g + GR, :], ps[6 + g][:, :], ACT.Copy).then_inc(s["xe"], 1)
                for g in range(NG):
                    act.wait_ge(s["wt"], v(2, g + 2))
                    act.activation(w_neg[:, GR * g:GR * g + GR, :], ps[2 + g][:, :], ACT.Copy, scale=-1.0)\
                        .then_inc(s["wneg"], 1)

                def o_out(p):
                    act.wait_ge(s["ot"], v(4, p + 2))
                    settle()
                    act.activation(big[:, 16 + 4 * p:20 + 4 * p, bass.ds((bi + 1) * P - P, P)],
                                   ps[6 + p % 2].rearrange("p (c t) -> p c t", t=P), ACT.Copy)\
                        .then_inc(s["oe"], 1)

                for p in range(4):
                    act.wait_ge(s["vn"], v(4, p + 2))
                    act.activation(vb[:, 2 * p:2 * p + 2, :], ps[4 + p % 2][:, :], ACT.Copy)\
                        .then_inc(s["vne"], 1)
                    if p:
                        o_out(p - 1)
                o_out(3)

            g0 = dn_gate0[l]
            kq = (EPS * P * 2 * P) ** 0.5

            def squares(h, i=0):
                n = HEADS * d + h + 2 * i
                if not (isinstance(i, int) and h == 0):
                    act.wait_ge(nss_done, n)
                else:
                    act.wait_ge(s["oe"], NB * 4 * (d + 1) + 1)
                    act.wait_ge(s["sst"], (NB + 1) * 8 * (d + 1))
                for c in range(2):
                    act.activation(nsq[:, c, :], big[:, 16 + 2 * h + c + 4 * i, :], ACT.Square).then_inc(nsq_done, 1)
                act.activation(nsq[:, 2, :], big[:, h + 2 * i, :], ACT.Square, scale=kq).then_inc(nsq_done, 1)

            def o_rstd(h, i=0):
                n = HEADS * d + h + 2 * i
                exp_and_ln()
                act.wait_ge(nss_done, n + 1)
                if not (isinstance(i, int) and h == 0):
                    act.wait_ge(on_done, 2 * n)
                act.activation(nr[:, :], ps[4][:, :], ACT.Ln, scale=1.0 / (2 * P), bias=EPS * P * EPS).then_inc(nln_done, 1)
                act.wait_ge(nln_done, n + 1)
                act.activation(nr[:, :], nr[:, :], ACT.Exp, scale=-0.5).then_inc(nr_done, 1)

            def gates(t, h, i=0):
                for c in range(2):
                    act.wait_ge(proj_done, 2 * t + c + 1 + 4 * i)
                    if not (isinstance(i, int) and h < 2):
                        act.wait_ge(yf_done, y_base[l] + 2 * h - 4 + c + 1 + 4 * i)
                    act.activation(gate[:, 2 * (h % 2) + c, :], bank(t, c)[:, :], ACT.Silu).then_inc(gate_done, 1)

            def y_his(h, i=0):
                for c in range(2):
                    k = 2 * h + c
                    act.wait_ge(yf_done, y_base[l] + k + 1 + 4 * i)
                    if isinstance(i, int):
                        dst = y_hi[:, y_at(k), :]
                    else:
                        dst = y_hi[:, k + 4 * i, :]
                    act.activation(dst, yf[:, 2 * (h % 2) + c, :], ACT.Copy).then_inc(yhi_done, 1)

            squares(0)
            for h in range(HEADS):
                t = g0 + h
                o_rstd(h)
                if h + 1 < HEADS:
                    squares(h + 1)
                hi(t + 1)
                if h:
                    if h == 1:
                        act.wait_ge(nsq_done, 3 * (HEADS * d + 2))
                    act.wait_ge(nsq_done, 3 * (HEADS * d + min(h + 2, HEADS)))
                    y_his(h - 1)
                gates(t, h)
            y_his(HEADS - 1)
            out_steps(l, g0 + 8, 8, 1)

        def stickbreak(l):
            n0, t0 = nth[l], tile_base[l]
            assert n0 == 0

            def v_step(t, i, k):
                if k or not isinstance(i, int):
                    hi(t + 1, i)
                for c in range(2):
                    act.wait_ge(proj_done, 2 * t + c + 1 + 4 * i)
                    w = 2 * P
                    settle()
                    act.activation(v_tok[:, 2 * c:2 * c + 2, bass.ds(w * k + 2 * w * i, w)],
                                   bank(t, c).rearrange("p (b n) -> p b n", b=2), ACT.Copy)\
                        .then_inc(proj_free, 1)

            walk(act, t0, 4, v_step)

            def square_qk(t, j, i=0):
                for c in range(2):
                    act.wait_ge(b["raw"], 2 * j + c + 1 + 4 * i)
                    if not (isinstance(i, int) and j == 0):
                        act.wait_ge(b["ss"], 2 * j - 1 + c + 4 * i)
                    act.activation(sb_sq[:, c, :], sb_raw[:, c, :], ACT.Square).then_inc(b["sq"], 1)

            def rms_qk(j, i=0):
                for c in range(2):
                    act.wait_ge(b["ss"], 2 * j + c + 1 + 4 * i)
                    if not (isinstance(i, int) and j == 0):
                        act.wait_ge(b["qk"], 2 * j - 1 + c + 4 * i)
                    act.activation(sb_r[:, c, :], ps[c][:, :], ACT.Ln, scale=1.0 / 64, bias=EPS).then_inc(proj_free, 1)
                    act.wait_ge(proj_free, 2 * (t0 + 4 + j) + c + 1 + 4 * i)
                    act.activation(sb_r[:, c, :], sb_r[:, c, :], ACT.Exp, scale=-0.5).then_inc(b["r"], 1)

            def softplus(u, j, i):
                n = 8 * j + u
                kb = 3 - u % 4
                w = T - P * kb
                zb, tt = ps[2 + u % 4][:, 0:w], sb_t[:, u % 2, 0:w]
                act.wait_ge(b["z"], n + 1 + 16 * i)
                if not (isinstance(i, int) and n < 2):
                    act.wait_ge(b["sp"], n - 1 + 16 * i)
                act.activation(tt, zb, ACT.Abs).then_inc(b["abs"], 1)
                act.wait_ge(b["abs"], n + 1 + 16 * i)
                act.activation(tt, tt, ACT.Exp, scale=-1.0).then_inc(b["exp"], 1)
                act.wait_ge(b["exp"], n + 1 + 16 * i)
                act.activation(tt, tt, ACT.Ln, bias=1.0).then_inc(b["ln1"], 1)

            def weights(n, i):
                u = n % 8
                kb = 3 - u % 4
                w = T - P * kb
                act.wait_ge(b["cum"], n + 1 + 16 * i)
                if not (isinstance(i, int) and n < 2):
                    act.wait_ge(b["pv"], n - 1 + 16 * i)
                act.activation(sb_w[:, u % 2, 0:w], ps[2 + u % 4][:, 0:w], ACT.Exp).then_inc(b["w"], 1)

            hi(t0 + 5)
            square_qk(t0 + 4, 0)
            rms_qk(0)

            def pair(j, i, first, last):
                t = t0 + 4 + j
                hi(t + 2, i)
                for u in range(8):
                    softplus(u, j, i)
                    if not (first and u < 2):
                        weights(8 * j + u - 2, i)
                    if u == 3 and not last:
                        square_qk(t + 1, j + 1, i)
                    if u == 4 and not last:
                        rms_qk(j + 1, i)

            pair(0, 0, True, False)
            with act.Fori(0, 3) as i:
                pair(1, i, False, False)
                pair(2, i, False, False)
            pair(7, 0, False, True)
            weights(62, 0)
            weights(63, 0)

            def y_his(k, i=0):
                for c in range(2):
                    n = 2 * k + c
                    act.wait_ge(yf_done, y_base[l] + n + 1 + 4 * i)
                    settle()
                    act.activation(y_hi[:, 8 + n + 4 * i, :], yf[:, 2 * (k % 2) + c, :], ACT.Copy).then_inc(yhi_done, 1)

            def gate_step(t, i, k):
                if not (isinstance(i, int) and k == 0):
                    hi(t + 1, i)
                for c in range(2):
                    act.wait_ge(proj_done, 2 * t + c + 1 + 4 * i)
                    if not (isinstance(i, int) and k < 2):
                        act.wait_ge(yf_done, y_base[l] + 2 * k - 4 + c + 1 + 4 * i)
                    act.activation(gate[:, 2 * (k % 2) + c, :], bank(t, c)[:, :], ACT.Silu).then_inc(b["gate"], 1)
                if not (isinstance(i, int) and k == 0):
                    y_his(k - 1, i)

            walk(act, t0 + 12, 4, gate_step)
            y_his(3)
            out_steps(l, t0 + 16, 4, 2)

        def shortconv(l):
            t0 = tile_base[l]

            def y_high(k, i=0):
                act.wait_ge(yf_done, y_base[l] + k + 1 + i)
                dst = y_hi[:, y_at(k), :] if isinstance(i, int) else y_hi[:, (k + 8) % 16 + i, :]
                settle()
                act.activation(dst, sc_yf[:, :], ACT.Copy).then_inc(yhi_done, 1)

            def group(j, i, first=False):
                t = t0 + 2 * j
                if not first:
                    hi(t + 1, i)
                    y_high(j - 1, i)
                act.wait_ge(proj_done, 2 * t + 1 + 4 * i)
                if not first:
                    act.wait_ge(c_["cu"], j + i)
                act.activation(sc_c[:, :], bank(t, 0)[:, :], ACT.Copy).then_inc(c_["c"], 1)
                hi(t + 2, i)
                act.wait_ge(proj_done, 2 * t + 4 + 4 * i)
                if not first:
                    act.wait_ge(yf_done, y_base[l] + j + i)
                act.activation(sc_gate[:, :], bank(t + 1, 1)[:, :], ACT.Silu).then_inc(c_["gate"], 1)

            group(0, 0, True)
            with act.Fori(0, 8) as i:
                group(1, i)
            with act.Fori(0, 7) as i:
                group(9, i)
            y_high(15)
            out_steps(l, t0 + 32, 8, 1)

        exp_and_ln()
        for m in range(KD):
            act.wait_ge(x_loaded[m // 2], 16)
            square_x(0, m)
        hi(0)
        for n in ACT_AHEAD:
            act.sem_inc(s[n], 1)
        for l, kind in enumerate(layers):
            norm(l)
            (deltanet, stickbreak, shortconv)[kind](l)

    @blk.vector
    def _(dve):
        def sum_squares(l, m, i=0, per=1):
            n = KD * l + m + 2 * per * i
            dve.wait_ge(sq_done, n + 1)
            if isinstance(i, int) and m == 0:
                if l:
                    dve.wait_ge(h_done, KD * l)
                dve.tensor_copy(rstd[:, :], sq[:, 0, :]).then_inc(sum_done, 1)
                return
            dve.wait_ge(sum_done, n - l)
            dve.tensor_tensor(rstd[:, :], rstd[:, :], sq[:, m % 2, :], ALU.add).then_inc(sum_done, 1)

        def norm(l):
            if l == 0:
                for m in range(KD - 1):
                    sum_squares(0, m)
                for m in range(KD // 2):
                    dve.wait_ge(x_loaded[m], 16)
                dve.wait_ge(loaded, 48)
            else:
                dve.wait_ge(x_done, KD * l)
            dve.wait_ge(rstd_done, l + 1)

            def low(k):
                dve.wait_ge(hhi_done, KD * l + k + 1)
                dve.tensor_tensor(h_lo[:, k, :], hf[:, k % 2, :], h_hi[:, k, :].bitcast(F32), ALU.subtract)\
                    .then_inc(h_done, 1)

            c0 = cols[l]["norm"]
            for k in range(KD):
                if k >= 2:
                    dve.wait_ge(h_done, KD * l + k - 1)
                dve.scalar_tensor_tensor(hf[:, k % 2, :], x[:, k, :], par[:, c0 + k:c0 + k + 1], rstd[:, :],
                                         ALU.mult, ALU.mult).then_inc(hf_done, 1)
                if k:
                    low(k - 1)
            low(KD - 1)

        def out_steps(l, first, n, per):
            if l == 0:
                dve.wait_ge(h_done, KD)

            def step(t, i, k):
                for c in range(per):
                    dve.wait_ge(proj_done, 2 * t + (c + 1 if per == 2 else 2) + 4 * i)
                    m = per * k + c + 2 * per * i
                    dve.tensor_tensor(x[:, m, :], bank(t, c)[:, :], x[:, m, :], ALU.add).then_inc(x_done, 1)
                    dve.wait_ge(x_done, KD * l + per * k + c + 1 + 2 * per * i)
                    dve.sem_inc(proj_free, 1 if per == 2 else 2)
                if l + 1 < len(layers) and not (isinstance(i, int) and k == 0):
                    for c in range(per):
                        sum_squares(l + 1, per * (k - 1) + c, i, per)

            walk(dve, first, n, step)
            if l + 1 < len(layers):
                for m in range(per * (n - 1), KD - 1):
                    sum_squares(l + 1, m)

        def y_lows(l, c, i, slot, k0=None):
            n = y_base[l] + c
            dve.wait_ge(yhi_done, n + 1 + i)

        def deltanet(l):
            d, t0, c0 = nth[l], tile_base[l], cols[l]
            bk = bank(t0, 0)
            v0, a0 = 9 * d, 6 * d
            dve.wait_ge(proj_done, 2 * (t0 + 1))
            dve.tensor_scalar(sp_b[0:8, :], bk[0:8, :], par[0:8, c0["dt"]:c0["dt"] + 1], 0.0, ALU.add, ALU.max)\
                .then_inc(dn_v, 1)
            dve.wait_ge(dn_a, a0 + 5)
            dve.wait_ge(dn_v, v0 + 1)
            dve.sem_inc(proj_free, 2)
            dve.tensor_tensor(sp_b[0:8, :], sp_b[0:8, :], sp_a[0:8, :], ALU.add).then_inc(dn_v, 1)
            dve.wait_ge(dn_v, v0 + 2)
            dve.tensor_scalar(sp_a[0:8, :], sp_b[0:8, :], bexp[0:8, 0:1], -1.0, ALU.mult, ALU.mult).then_inc(dn_v, 1)
            dve.wait_ge(dn_v, v0 + 3)
            if d == 0:
                dve.wait_ge(zeroed, 1)
            for n in range(NB):
                dve.tensor_tensor_scan(rows[0:8, n * P:n * P + P], cf[0:8, C_ONES:C_ONES + P],
                                       sp_a[0:8, n * P:n * P + P], 0.0, ALU.mult, ALU.add).then_inc(dn_v, 1)
            dve.tensor_scalar(sp_c[32:40, :], sp_c[32:40, :], 1.0, None, ALU.add).then_inc(dn_v, 1)
            dve.wait_ge(dn_v, v0 + 8)
            g4 = rows[0:8, :].rearrange("p (n t) -> p n t", t=P)
            dve.tensor_tensor(sp_b[0:8, :].rearrange("p (n t) -> p n t", t=P), g4[:, :, P - 1:P].to_broadcast([8, NB, P]),
                              g4, ALU.subtract).then_inc(dn_v, 1)
            dve.reciprocal(rows[32:40, :], sp_c[32:40, :]).then_inc(s["gend"], 1)

            def step(t, i, k):
                for c in range(2):
                    n = 32 * d + 2 * k + c
                    a = acc[:, 2 * (k % 2) + c, :]
                    bk = bank(t, c)

                    def w(j):
                        if isinstance(i, int):
                            at_ = c0["conv"] + 4 * (2 * k + c) + j
                            return par[:, at_:at_ + 1]
                        return par[:, bass.ds(16 * i + (c0["conv"] + 4 * (2 * k + c) + j), 1)]

                    dve.wait_ge(proj_done, 2 * t + c + 1 + 4 * i)
                    if not (isinstance(i, int) and k < 2):
                        dve.wait_ge(silu_done, n - 3 + 4 * i)
                    dve.tensor_scalar(a, bk[:, :], w(3), None, ALU.mult).then_inc(conv_step, 1)
                    for j in (1, 2):
                        dve.wait_ge(conv_step, 3 * n + j + 12 * i)
                        dve.scalar_tensor_tensor(a[:, j:T], bk[:, 0:T - j], w(3 - j), a[:, j:T], ALU.mult, ALU.add)\
                            .then_inc(conv_step, 1)
                    dve.wait_ge(conv_step, 3 * n + 3 + 12 * i)
                    dve.scalar_tensor_tensor(a[:, 3:T], bk[:, 0:T - 3], w(0), a[:, 3:T], ALU.mult, ALU.add)\
                        .then_inc(conv_done, 1)
                    dve.wait_ge(conv_done, n + 1 + 4 * i)
                    dve.sem_inc(proj_free, 1)

            def split_row(q):
                own = slice(32 * q, 32 * q + 8)
                part = [slice(32 * ((q + j) % 3), 32 * ((q + j) % 3) + 8) for j in range(3)]
                n = 12 * d + 4 * q
                dve.tensor_copy(row_parts[own, q, :], rows[own, :]).then_inc(part_step, 1)
                dve.wait_ge(part_step, n + 1)
                dve.tensor_tensor(sp_c[own, :], rows[own, :], row_parts[own, q, :], ALU.subtract).then_inc(part_step, 1)
                dve.wait_ge(part_step, n + 2)
                dve.tensor_copy(mid[own, :], sp_c[own, :]).then_inc(part_step, 1)
                dve.tensor_copy(row_parts[part[1], q, :], sp_c[own, :]).then_inc(part_step, 1)
                dve.wait_ge(part_step, n + 4)
                dve.tensor_tensor(row_parts[part[2], q, :], sp_c[own, :], mid[own, :], ALU.subtract).then_inc(parts_done, 1)

            def step_and_rows(t, i, k):
                step(t, i, k)
                if isinstance(i, int) and k < 2:
                    if k == 0:
                        dve.wait_ge(dn_v, v0 + 9)
                        if d == 0:
                            dve.wait_ge(zeroed, 2)
                    else:
                        dve.wait_ge(s["gend"], (NB + 1) * d + 1)
                    split_row(k)

            walk(dve, t0 + 1, 12, step_and_rows)
            step(t0 + 13, 0, 12)
            dve.wait_ge(s["sz"], 2 * d + 2)
            split_row(2)
            for k in range(13, 16):
                step(t0 + 1 + k, 0, k)
            dve.wait_ge(silu_done, 32 * d + 32)
            dve.memset(state[:, :, :], 0.0).then_inc(s["sst"], 8)

            with dve.Fori(0, NB) as bi:
                def v(per, k):
                    return NB * d * per + bi * per + k

                def gr(t, g):
                    return t[:, GR * g:GR * g + GR, :]

                def bk(n, w=P):
                    return ps[n].rearrange("p (h t) -> p h t", t=w)

                for g in range(NG):
                    dve.wait_ge(s["rkbc"], v(2, g + 1))
                    dve.wait_ge(s["wt"], v(2, 1))
                    dve.tensor_tensor(gr(kn, g), bk(2 + g), big[:, 8 + GR * g:8 + GR * g + GR, bass.ts(bi, P)], ALU.mult)\
                        .then_inc(s["kn"], 1)
                dve.wait_ge(s["tokt"], v(1, 2))
                dve.tensor_copy(tok[:, :], ps[6][:, 0:P]).then_inc(s["tok"], 1)
                for g in range(NG):
                    dve.wait_ge(s["bbc"], v(2, g + 1))
                    dve.wait_ge(s["kn"], v(2, g + 1))
                    dve.tensor_tensor(gr(k_beta, g), bk(4 + g), gr(kn, g), ALU.mult).then_inc(s["kbeta"], 1)
                    if g == 0:
                        dve.wait_ge(s["tok"], v(1, 1))
                        dve.tensor_scalar(tok_neg[:, :], tok[:, 0:8], -1.0, None, ALU.mult).then_inc(s["tokneg"], 1)

                def beta_v(p):
                    dve.wait_ge(s["vt"], v(4, p + 1))
                    dve.wait_ge(s["su"], v(4, 1))
                    bank_ = ps[(7, 6, 2, 3)[p]].rearrange("p (h t) -> p h t", t=2 * P)
                    dve.tensor_tensor(vb[:, 2 * p:2 * p + 2, :], bank_,
                                      tok[:, 32 + 2 * p:34 + 2 * p].unsqueeze(2).to_broadcast([P, 2, 2 * P]), ALU.mult)\
                        .then_inc(s["vb"], 1)

                beta_v(0)
                beta_v(1)
                for g in range(NG):
                    dve.wait_ge(s["kk"], v(2, g + 1))
                    dve.wait_ge(s["dec"], v(8, GR * g + GR))
                    dve.wait_ge(s["vt"], v(4, 4))
                    dve.tensor_tensor(gr(l_t, g), bk(4 + g), gr(attn_t, g), ALU.mult).then_inc(s["lt"], 1)
                sub = cb[:, B_SUB:B_SUB + P].unsqueeze(1).to_broadcast([P, GR, P])
                idb = ident.unsqueeze(1).to_broadcast([P, GR, P])
                for g in range(NG):
                    dve.wait_ge(s["lt"], v(2, g + 1))
                    dve.tensor_tensor(gr(inv_t, g), gr(l_t, g), sub, ALU.mult).then_inc(s["u0"], 1)
                for g in range(NG):
                    dve.wait_ge(s["u0"], v(2, g + 1))
                    dve.tensor_tensor(gr(inv_t, g), gr(inv_t, g), idb, ALU.add).then_inc(s["u0i"], 1)
                beta_v(2)
                beta_v(3)
                for g in range(NG):
                    dve.wait_ge(s["qk"], v(2, g + 1))
                    dve.tensor_tensor(gr(attn_t, g), bk(7 - g), gr(attn_t, g), ALU.mult).then_inc(s["at"], 1)
                n_l = LEVELS - 1
                for lv in range(n_l):
                    mask = cb[:, B_LEVEL + lv * P:B_LEVEL + lv * P + P].unsqueeze(1).to_broadcast([P, GR, P])
                    for g in range(NG):
                        dve.wait_ge(s["pm"], v(2 * n_l, 2 * lv + g + 1))
                        dve.tensor_tensor(gr(prod, g), bk(2 + g), mask, ALU.mult).then_inc(s["pe_p"], 1)
                    if lv == 1:
                        dve.wait_ge(s["eg"], v(2, 2))
                        dve.wait_ge(s["sst"], NB * d * 8 + 8 * d + 8 + bi * 8)
                        dve.tensor_copy(g_end[:, :], decay[:, :, P - 1]).then_inc(s["gend"], 1)
                        dve.wait_ge(s["tokexp"], v(1, 1))
                        dve.tensor_tensor(bexp[:, :], bexp[:, :], tok[:, 32:40], ALU.mult).then_inc(s["bexp"], 1)
                    for g in range(NG):
                        dve.wait_ge(s["du"], v(2 * n_l, 2 * lv + g + 1))
                        if lv:
                            dve.wait_ge(s["ue"], v(2 * n_l, 2 * lv + g - 1))
                        else:
                            dve.wait_ge(s["u0i"], v(2, g + 1))
                        dve.tensor_tensor(gr(inv_t, g), gr(inv_t, g), bk(4 + g), ALU.subtract).then_inc(s["ue"], 1)
                for g in range(NG):
                    dve.wait_ge(s["ktok"], v(2, g + 1))
                    dve.wait_ge(s["pm"], v(2 * n_l, 2 * n_l))
                    dve.wait_ge(s["bexp"], v(1, 1))
                    dve.tensor_tensor(gr(k_in, g), bk(g), bexp[:, GR * g:GR * g + GR].unsqueeze(2).to_broadcast([P, GR, P]),
                                      ALU.mult).then_inc(s["kin"], 1)
                for g in range(NG):
                    dve.tensor_tensor(gr(k_out, g), bk(g),
                                      tok[:, 96 + GR * g:96 + GR * g + GR].unsqueeze(2).to_broadcast([P, GR, P]),
                                      ALU.mult).then_inc(s["kout"], 1)
                for h in range(HEADS):
                    p = h // 2
                    if h == 0:
                        dve.wait_ge(s["gend"], NB * d + d + 2 + bi)
                    if h % 2 == 0:
                        dve.wait_ge(s["ot0"], v(4, p + 1))
                        dve.wait_ge(s["su"], v(4, p + 2))
                    dve.scalar_tensor_tensor(state[:, h, :], state[:, h, :], g_end[:, h:h + 1],
                                             ps[p % 2][:, (h % 2) * 2 * P:(h % 2 + 1) * 2 * P], ALU.mult, ALU.add)\
                        .then_inc(s["sst"], 1)

            co = c0["onorm"]

            def sum_norm(h):
                n = HEADS * d + h
                for c in (1, 2):
                    dve.wait_ge(nsq_done, 3 * n + c + 1)
                    if c == 2:
                        dve.wait_ge(nsum_done, 2 * n + 1)
                    dve.tensor_tensor(nsq[:, 0, :], nsq[:, 0, :], nsq[:, c, :], ALU.add).then_inc(nsum_done, 1)

            sum_norm(0)
            for h in range(HEADS):
                n = HEADS * d + h
                if h + 1 < HEADS:
                    sum_norm(h + 1)
                for c in range(2):
                    ob = big[:, 16 + 2 * h + c, :]
                    dve.wait_ge(nr_done, n + 1)
                    dve.scalar_tensor_tensor(ob, ob, par[:, co + c:co + c + 1], nr[:, :], ALU.mult, ALU.mult)\
                        .then_inc(on_done, 1)
                for c in range(2):
                    k = y_base[l] + 2 * h + c
                    dve.wait_ge(gate_done, 2 * n + c + 1)
                    dve.wait_ge(on_done, 2 * n + c + 1)
                    if h >= 2:
                        dve.wait_ge(y_done, k - 3)
                    slot = 2 * (h % 2) + c
                    dve.tensor_tensor(yf[:, slot, :], big[:, 16 + 2 * h + c, :], gate[:, slot, :], ALU.mult)\
                        .then_inc(yf_done, 1)
                    dve.sem_inc(proj_free, 1)
                if h:
                    y_lows2(l, h - 1)
            y_lows2(l, HEADS - 1)
            out_steps(l, dn_gate0[l] + 8, 8, 1)

        def y_lows2(l, h, i=0):
            for c in range(2):
                n = 2 * h + c
                slot = 2 * (h % 2) + c
                dve.wait_ge(yhi_done, y_base[l] + n + 1 + 4 * i)
                if isinstance(i, int):
                    hi_b, lo_b = y_hi[:, y_at(n), :], y_lo[:, n, :]
                else:
                    hi_b, lo_b = y_hi[:, 8 + n + 4 * i, :], y_lo[:, n + 4 * i, :]
                dve.tensor_tensor(lo_b, yf[:, slot, :], hi_b.bitcast(F32), ALU.subtract).then_inc(y_done, 1)

        def stickbreak(l):
            t0, c0 = tile_base[l], cols[l]
            dve.sem_inc(b["ev"], 1)
            dve.tensor_scalar(gq8[:, :], par[:, c0["q"]:c0["q"] + 1], 0.125, None, ALU.mult).then_inc(b["gq8"], 1)

            def raws(t, j, i=0):
                for c in range(2):
                    dve.wait_ge(proj_done, 2 * t + c + 1 + 4 * i)
                    if not (isinstance(i, int) and j == 0):
                        dve.wait_ge(b["qk"], 2 * j - 1 + c + 4 * i)
                    dve.tensor_copy(sb_raw[:, c, :], ps[c][:, :]).then_inc(b["raw"], 1)

            def scaled(j, i=0):
                par_ = j % 2
                for c, gain in enumerate((gq8[:, 0:1], par[:, c0["k"]:c0["k"] + 1])):
                    dve.wait_ge(b["r"], 2 * j + c + 1 + 4 * i)
                    dve.wait_ge(b["raw"], 2 * j + c + 1 + 4 * i)
                    if j == 0 and isinstance(i, int) and c == 0:
                        dve.wait_ge(b["gq8"], 1)
                    if not (isinstance(i, int) and j < 2):
                        dve.wait_ge(b["z"], 8 * (j - 1) + 16 * i)
                    dve.scalar_tensor_tensor(sb_qk[:, par_, c, :], sb_raw[:, c, :], gain, sb_r[:, c, :],
                                             ALU.mult, ALU.mult).then_inc(b["qk"], 1)
                if not (isinstance(i, int) and j < 2):
                    dve.wait_ge(b["pv"], 8 * (j - 1) + 16 * i)
                if isinstance(i, int):
                    src = v_tok[:, :, j * P:j * P + P]
                else:
                    src = v_tok[:, :, bass.ds(2 * P * i + j * P, P)]
                dve.tensor_copy(sb_v[:, par_, :, :], src).then_inc(b["v"], 1)

            def softplus(u, j, i):
                n = 8 * j + u
                kb = 3 - u % 4
                w = T - P * kb
                off = (0, 128, 384, 768)[u % 4]
                dve.wait_ge(b["ln1"], n + 1 + 16 * i)
                if not (isinstance(i, int) and n < 8):
                    dve.wait_ge(b["cum"], 8 * j + 4 * (u // 4) - 4 + 16 * i)
                dve.scalar_tensor_tensor(sb_sp[:, u // 4, off:off + w], ps[2 + u % 4][:, 0:w], 0.0,
                                         sb_t[:, u % 2, 0:w], ALU.max, ALU.add).then_inc(b["sp"], 1)

            dve.wait_ge(proj_free, 2 * (t0 + 4))
            raws(t0 + 4, 0)
            scaled(0)

            def evac(j, i):
                dve.wait_ge(b["pv"], 8 * j + 8 + 16 * i)
                dst = o_sb[:, j, :] if isinstance(i, int) else o_sb[:, j + 2 * i, :]
                dve.tensor_copy(dst, ps[6 + j % 2][:, :]).then_inc(b["ev"], 1)

            def pair(j, i, first, last):
                t = t0 + 4 + j
                for u in range(8):
                    softplus(u, j, i)
                    if u == 2 and not last:
                        raws(t + 1, j + 1, i)
                    if u == 4 and not first:
                        evac(j - 1, i)
                    if u == 5 and not last:
                        scaled(j + 1, i)

            pair(0, 0, True, False)
            with dve.Fori(0, 3) as i:
                pair(1, i, False, False)
                pair(2, i, False, False)
            pair(7, 0, False, True)
            evac(7, 0)

            def gate_step(t, i, k):
                for c in range(2):
                    n = 2 * k + c
                    slot = 2 * (k % 2) + c
                    dve.wait_ge(b["gate"], n + 1 + 4 * i)
                    if not (isinstance(i, int) and k < 2):
                        dve.wait_ge(y_done, y_base[l] + n - 3 + 4 * i)
                    if isinstance(i, int) and k == 0:
                        dve.wait_ge(b["ev"], 8)
                    dve.tensor_tensor(yf[:, slot, :], o_sb[:, n + 4 * i, :], gate[:, slot, :], ALU.mult).then_inc(yf_done, 1)
                    dve.sem_inc(proj_free, 1)
                if not (isinstance(i, int) and k == 0):
                    y_lows2(l, k - 1, i)

            walk(dve, t0 + 12, 4, gate_step)
            y_lows2(l, 3)
            out_steps(l, t0 + 16, 4, 2)

        def shortconv(l):
            t0, cw = tile_base[l], cols[l]["conv"]
            dve.memset(sc_cu[:, 0:2], 0.0).then_inc(c_["zero"], 1)
            dve.wait_ge(c_["zero"], 1)

            def low(k, i=0):
                dve.wait_ge(yhi_done, y_base[l] + k + 1 + i)
                src = y_hi[:, y_at(k), :] if isinstance(i, int) else y_hi[:, (k + 8) % 16 + i, :]
                dve.tensor_tensor(y_lo[:, k + i, :], sc_yf[:, :], src.bitcast(F32), ALU.subtract).then_inc(y_done, 1)

            def group(j, i, first=False):
                t = t0 + 2 * j
                dve.wait_ge(c_["c"], j + 1 + i)
                dve.wait_ge(proj_done, 2 * t + 2 + 4 * i)
                if not first:
                    dve.wait_ge(c_["conv"], j + i)
                dve.tensor_tensor(sc_cu[:, 2:T + 2], bank(t, 1)[:, :], sc_c[:, :], ALU.mult).then_inc(c_["cu"], 1)
                dve.wait_ge(c_["cu"], j + 1 + i)
                dve.sem_inc(proj_free, 2)
                if not first:
                    dve.wait_ge(c_["y"], j + i)

                def w(m):
                    if isinstance(i, int):
                        return par[:, cw + 3 * j + m:cw + 3 * j + m + 1]
                    return par[:, bass.ds(3 * i + (cw + 3 * j + m), 1)]

                n = 2 * j + 2 * i
                dve.tensor_scalar(sc_acc[:, :], sc_cu[:, 2:T + 2], w(2), None, ALU.mult).then_inc(c_["cstep"], 1)
                dve.wait_ge(c_["cstep"], n + 1)
                dve.scalar_tensor_tensor(sc_acc[:, :], sc_cu[:, 1:T + 1], w(1), sc_acc[:, :], ALU.mult, ALU.add)\
                    .then_inc(c_["cstep"], 1)
                dve.wait_ge(c_["cstep"], n + 2)
                dve.scalar_tensor_tensor(sc_acc[:, :], sc_cu[:, 0:T], w(0), sc_acc[:, :], ALU.mult, ALU.add)\
                    .then_inc(c_["conv"], 1)
                if not first:
                    low(j - 1, i)
                dve.wait_ge(c_["conv"], j + 1 + i)
                dve.wait_ge(proj_done, 2 * t + 3 + 4 * i)
                if not first:
                    dve.wait_ge(yf_done, y_base[l] + j + i)
                dve.tensor_tensor(sc_y[:, :], bank(t + 1, 0)[:, :], sc_acc[:, :], ALU.mult).then_inc(c_["y"], 1)
                dve.wait_ge(c_["y"], j + 1 + i)
                dve.wait_ge(c_["gate"], j + 1 + i)
                dve.sem_inc(proj_free, 2)
                if not first:
                    dve.wait_ge(y_done, y_base[l] + j + i)
                dve.tensor_tensor(sc_yf[:, :], sc_y[:, :], sc_gate[:, :], ALU.mult).then_inc(yf_done, 1)

            group(0, 0, True)
            with dve.Fori(0, 8) as i:
                group(1, i)
            with dve.Fori(0, 7) as i:
                group(9, i)
            low(15)
            out_steps(l, t0 + 32, 8, 1)

        for l, kind in enumerate(layers):
            norm(l)
            (deltanet, stickbreak, shortconv)[kind](l)

    @blk.tensor
    def _(pe):
        def passes(out_, w_h, w_l, m_h, m_l, start, stop):
            pe.matmul(out_, w_h, m_h, start=start, stop=False)
            pe.matmul(out_, w_h, m_l, start=False, stop=False)
            return pe.matmul(out_, w_l, m_h, start=False, stop=stop)

        def ready(t, i=0):
            pe.wait_ge(lo_done, t + 1 + 2 * i)
            if not (isinstance(i, int) and t < 2):
                pe.wait_ge(proj_free, 2 * (t - 1) + 4 * i)

        def in_block(t, c, k, bk=None, width=2 * P):
            bk = bank(t, c) if bk is None else bk
            w = slice(k * 2 * P + c * P, k * 2 * P + c * P + P)
            return passes(bk[:, :], w_hi[:, t % 2, w], w_lo[:, t % 2, w], h_hi[:, k, :], h_lo[:, k, :],
                          k == 0, k == KD - 1)

        def in_tile(t, i=0):
            ready(t, i)
            for c in range(2):
                for k in range(KD):
                    mm = in_block(t, c, k)
                mm.then_inc(proj_done, 1)

        def first_tiles(l, t, chunks):
            ready(t)
            ready(t + 1)
            for k in range(KD):
                pe.wait_ge(h_done, KD * l + k + 1)
                for t_, c, n in chunks:
                    mm = in_block(t_, c, k)
                    if k == KD - 1:
                        mm.then_inc(proj_done, n)

        def sum_x(l):
            pe.wait_ge(sum_done, (KD - 1) * (l + 1))
            pe.matmul(ps[7][:, :], ones, rstd[:, :], start=True, stop=False)
            pe.wait_ge(sq_done, KD * (l + 1))
            pe.matmul(ps[7][:, :], ones, sq[:, (KD - 1) % 2, :], start=False, stop=True).then_inc(ss_done, 1)

        def out_steps(l, first, n, per):
            more = l + 1 < len(layers)

            def step(t, i, k):
                ready(t, i)
                first_step = isinstance(i, int) and k == 0
                for c in range(per):
                    kn_ = 16 // per
                    for kk in range(kn_):
                        if first_step and c == 0:
                            pe.wait_ge(y_done, y_base[l] + kk + 1)
                        w = slice(kk * per * P + c * P, kk * per * P + c * P + P)
                        mm = passes(bank(t, c)[:, :], w_hi[:, t % 2, w], w_lo[:, t % 2, w],
                                    y_hi[:, y_at(kk), :], y_lo[:, kk, :], kk == 0, kk == kn_ - 1)
                    mm.then_inc(proj_done, 2 // per)
            walk(pe, first, n, step)
            if more:
                sum_x(l + 1)

        def deltanet(l):
            d, t0 = nth[l], tile_base[l]
            first_tiles(l, t0, [(t0, 0, 2), (t0 + 1, 0, 1), (t0 + 1, 1, 1)])
            in_tile(t0 + 2)
            with pe.Fori(0, 3) as i:
                in_tile(t0 + 3, i)
                in_tile(t0 + 4, i)

            for k in range(HEADS // 2):
                in_tile(t0 + 9 + k)
                for h in (2 * k, 2 * k + 1):
                    pe.wait_ge(ksq_done, HEADS * d + h + 1)
                    sel = cf[:, C_SELK + 8 * h:C_SELK + 8 * h + 8]
                    pe.matmul(ps[7][0:8, :], sel, ksq[:, h % 2, :], start=(h == 0), stop=(h == HEADS - 1))\
                        .then_inc(kss_done, 1)
            for k in range(4):
                in_tile(t0 + 13 + k)

            def spread(q, bk, g, block_):
                for h in range(GR):
                    hh = GR * g + h
                    mm = pe.matmul(bk[:, h * P:h * P + P], cb[0:96, B_SEL + hh * P:B_SEL + hh * P + P],
                                   row_parts[0:96, q, block_], start=(h == 0), stop=(h == GR - 1),
                                   skip_group_check=True)
                return mm

            def convolved(n):
                last = t0 + 16
                return 2 * last + (n % 2 + 1 if n // 2 == last % 2 else 0)

            with pe.Fori(0, NB) as bi:
                def v(per, k):
                    return NB * d * per + bi * per + k

                n_l = LEVELS - 1
                now = bass.ts(bi, P)
                pe.wait_ge(parts_done, 3 * d + 3)
                for g in range(NG):
                    pe.wait_ge(s["vne"], v(4, 1))
                    spread(1, ps[4 + g], g, now).then_inc(s["bbc"], 1)
                for g in range(NG):
                    pe.wait_ge(s["wneg"], v(2, 1))
                    pe.wait_ge(proj_free, convolved(2 + g))
                    spread(2, ps[2 + g], g, now).then_inc(s["rkbc"], 1)
                for g in range(NG):
                    pe.wait_ge(s["sst"], NB * d * 8 + 8 * d + 8 + bi * 8)
                    pe.wait_ge(proj_free, convolved(g))
                    spread(0, ps[g], g, now).then_inc(s["gbc"], 1)
                    pe.matmul(ps[g][:, :], cb[:, B_ID:B_ID + P],
                              cb[:, B_INCL:B_INCL + P].unsqueeze(1).to_broadcast([P, GR, P]),
                              start=False, stop=True, skip_group_check=True).then_inc(s["gmask"], 1)
                pe.wait_ge(s["rows_b"], v(1, 1))
                pe.wait_ge(s["oe"], v(4, 1))
                pe.transpose(ps[6][:, 0:P], rows_b[:, :], ident).then_inc(s["tokt"], 1)

                def v_turn(p):
                    bk = ps[(7, 6, 2, 3)[p]]
                    src = prod if p < 2 else l_t
                    pe.wait_ge(s["vstage"] if p < 2 else s["vstage2"], v(1, 1))
                    for c in range(4):
                        mm = pe.transpose(bk[:, c * P:c * P + P], src[:, 4 * (p % 2) + c, :], ident)
                    mm.then_inc(s["vt"], 1)

                v_turn(0)
                pe.wait_ge(s["tok"], v(1, 1))
                v_turn(1)
                for g in range(NG):
                    pe.wait_ge(s["kbeta"], v(2, g + 1))
                    for h in range(GR):
                        mm = pe.matmul(ps[4 + g][:, h * P:h * P + P], kn[:, GR * g + h, :], k_beta[:, GR * g + h, :],
                                       start=True, stop=True)
                    mm.then_inc(s["kk"], 1)
                v_turn(2)
                v_turn(3)
                for g in range(NG):
                    pe.wait_ge(s["vb"], v(4, g + 1))
                    for h in range(GR):
                        mm = pe.matmul(ps[7 - g][:, h * P:h * P + P], kn[:, GR * g + h, :],
                                       big[:, GR * g + h, bass.ts(bi, P)], start=True, stop=True)
                    mm.then_inc(s["qk"], 1)
                for g in range(NG):
                    pe.wait_ge(s["u0i"], v(2, g + 1))
                    pe.wait_ge(s["dec"], v(8, GR * g + GR))
                    for h in range(GR):
                        mm = pe.transpose(ps[g][:, h * P:h * P + P], inv_t[:, GR * g + h, :], ident)
                    mm.then_inc(s["xt"], 1)
                for g in range(NG):
                    pe.wait_ge(s["lt"], v(2, g + 1))
                    spread(0, ps[4 + g], g, now).then_inc(s["gbc2"], 1)
                for lv in range(n_l):
                    for g in range(NG):
                        if lv == 0:
                            pe.wait_ge(s["x0"], v(2, g + 1))
                            pe.wait_ge(s["vb"], v(4, 3 + g))
                        else:
                            pe.wait_ge(s["xe"], v(2 * (n_l - 1), 2 * lv + g - 1))
                        for h in range(GR):
                            mm = pe.matmul(ps[2 + g][:, h * P:h * P + P], l_t[:, GR * g + h, :], inv[:, GR * g + h, :],
                                           start=True, stop=True)
                        mm.then_inc(s["pm"], 1)
                    if lv == 0:
                        for g in range(NG):
                            pe.wait_ge(s["x0"], v(2, g + 1))
                            for h in range(GR):
                                mm = pe.transpose(ps[g][:, h * P:h * P + P], kn[:, GR * g + h, :], ident)
                            mm.then_inc(s["ktok"], 1)
                    for g in range(NG):
                        pe.wait_ge(s["pe_p"], v(2 * n_l, 2 * lv + g + 1))
                        if lv:
                            pe.wait_ge(s["ue"], v(2 * n_l, 2 * lv + g - 1))
                        else:
                            pe.wait_ge(s["eg"], v(2, g + 1))
                        for h in range(GR):
                            mm = pe.matmul(ps[4 + g][:, h * P:h * P + P], prod[:, GR * g + h, :], inv_t[:, GR * g + h, :],
                                           start=True, stop=True)
                        mm.then_inc(s["du"], 1)
                    if lv < n_l - 1:
                        for g in range(NG):
                            pe.wait_ge(s["ue"], v(2 * n_l, 2 * lv + g + 1))
                            if lv == 0:
                                pe.wait_ge(s["at"], v(2, 2 - g))
                            for h in range(GR):
                                mm = pe.transpose(ps[6 + g][:, h * P:h * P + P], inv_t[:, GR * g + h, :], ident)
                            mm.then_inc(s["turned"], 1)
                def state_out(p):
                    if p >= 2:
                        pe.wait_ge(s["oe"], v(4, p))
                    for e in range(2):
                        h = 2 * p + e
                        for c in range(2):
                            o_ = ps[6 + p % 2][:, (2 * e + c) * P:(2 * e + c + 1) * P]
                            mm = pe.matmul(o_, state[:, h, c * P:c * P + P], q_dec[:, h, :], start=(e == 0 and c == 0),
                                           stop=False, skip_group_check=True)
                    mm.then_inc(s["ot0"], 1)

                pe.wait_ge(s["qdec"], v(2, 2))
                pe.wait_ge(s["xe"], v(2 * (n_l - 1), 2 * (n_l - 1)))
                state_out(0)
                state_out(1)
                for g in range(NG):
                    pe.wait_ge(s["kin"], v(2, g + 1))
                    pe.wait_ge(s["ue"], v(2 * n_l, 2 * n_l - 1 + g))
                    for h in range(GR):
                        mm = pe.matmul(ps[2 + g][:, h * P:h * P + P], k_in[:, GR * g + h, :], inv_t[:, GR * g + h, :],
                                       start=True, stop=True)
                    mm.then_inc(s["wt"], 1)

                def v_new(p):
                    if p < 2:
                        pe.wait_ge(s["wneg"], v(2, p // 2 + 2))
                        pe.wait_ge(s["ue"], v(2 * n_l, 2 * n_l))
                    else:
                        pe.wait_ge(s["wneg"], v(2, 3))
                        pe.wait_ge(s["vne"], v(4, p))
                    for e in range(2):
                        h = 2 * p + e
                        o_ = ps[4 + p % 2][:, e * 2 * P:(e + 1) * 2 * P]
                        pe.matmul(o_, inv_t[:, h, :], vb[:, h, :], start=True, stop=False)
                        mm = pe.matmul(o_, w_neg[:, h, :], state[:, h, :], start=False, stop=True)
                    mm.then_inc(s["vn"], 1)

                def o_t(p):
                    pe.wait_ge(s["vne"], v(4, p + 2))
                    pe.wait_ge(s["kout"], v(2, 2))
                    if p >= 2:
                        pe.wait_ge(s["sst"], NB * d * 8 + 8 * d + 8 + bi * 8 + 2 * (p - 1))
                    for e in range(2):
                        h = 2 * p + e
                        mm = pe.matmul(ps[p % 2][:, e * 2 * P:(e + 1) * 2 * P], k_out[:, h, :], vb[:, h, :],
                                       start=True, stop=True)
                    mm.then_inc(s["su"], 1)
                    for e in range(2):
                        h = 2 * p + e
                        for c in range(2):
                            o_ = ps[6 + p % 2][:, (2 * e + c) * P:(2 * e + c + 1) * P]
                            mm = pe.matmul(o_, vb[:, h, c * P:c * P + P], attn_t[:, h, :], start=False, stop=True,
                                           skip_group_check=True)
                    mm.then_inc(s["ot"], 1)

                v_new(0)
                for p in range(4):
                    if p < 3:
                        v_new(p + 1)
                    if p >= 2:
                        state_out(p)
                    o_t(p)

            for h in range(HEADS):
                n = HEADS * d + h
                pe.wait_ge(nsum_done, 2 * n + 2)
                if h:
                    pe.wait_ge(nln_done, n)
                pe.matmul(ps[4][:, :], ones, nsq[:, 0, :], start=True, stop=True).then_inc(nss_done, 1)
                in_tile(dn_gate0[l] + h)
            out_steps(l, dn_gate0[l] + 8, 8, 1)

        def stickbreak(l):
            t0 = tile_base[l]

            def v_part(t, tb, k_, start):
                o_ = bank(t, tb // 2)[:, (tb % 2) * 2 * P:(tb % 2 + 1) * 2 * P]
                tk = slice(tb * P, tb * P + P)
                w = slice(k_ * 2 * P, (k_ + 1) * 2 * P)
                hh, hl, wh, wl = h_hi[:, k_, tk], h_lo[:, k_, tk], w_hi[:, t % 2, w], w_lo[:, t % 2, w]
                last = k_ == KD - 1
                pe.matmul(o_, hh, wh, start=start, stop=False, skip_group_check=True)
                pe.matmul(o_, hh, wl, start=False, stop=False, skip_group_check=True)
                return pe.matmul(o_, hl, wh, start=False, stop=last, skip_group_check=True)

            ready(t0)
            ready(t0 + 1)
            for k_ in range(KD):
                pe.wait_ge(h_done, KD * l + k_ + 1)
                for t in (t0, t0 + 1):
                    for tb in range(NB):
                        mm = v_part(t, tb, k_, k_ == 0 and tb % 2 == 0)
                        if k_ == KD - 1 and tb % 2:
                            mm.then_inc(proj_done, 1)
            for t in (t0 + 2, t0 + 3):
                ready(t)
                for tb in range(NB):
                    for k_ in range(KD):
                        mm = v_part(t, tb, k_, k_ == 0)
                    if tb % 2:
                        mm.then_inc(proj_done, 1)

            def qk_ready(t, i):
                pe.wait_ge(lo_done, t + 1 + 2 * i)
                pe.wait_ge(proj_free, 2 * t + 4 * i)

            def qk_part(t, i, c, k):
                mm = in_block(t, c, k, bk=ps[c])
                if k == KD - 1:
                    mm.then_inc(proj_done, 1)

            def sums(j, i=0):
                for c in range(2):
                    pe.wait_ge(b["sq"], 2 * j + c + 1 + 4 * i)
                    pe.wait_ge(b["raw"], 2 * j + c + 1 + 4 * i)
                    pe.matmul(ps[c][:, :], cf[:, C_BLOCK:C_BLOCK + P], sb_sq[:, c, :], start=True, stop=True)\
                        .then_inc(b["ss"], 1)

            qk_ready(t0 + 4, 0)
            for c in range(2):
                for k in range(KD):
                    qk_part(t0 + 4, 0, c, k)
            sums(0)

            def geometry(u):
                kb = 3 - u % 4
                return kb, T - P * kb, u // 4

            def z(u, j, i):
                n = 8 * j + u
                kb, w, e = geometry(u)
                qs = slice(kb * P, T)
                rr = slice(64 * e, 64 * e + 64)
                bk = ps[2 + u % 4]
                if u == 0:
                    pe.wait_ge(b["qk"], 2 * j + 2 + 4 * i)
                    pe.wait_ge(b["v"], j + 1 + 2 * i)
                if not (isinstance(i, int) and n < 4):
                    pe.wait_ge(b["w"], n - 3 + 16 * i)
                pe.matmul(bk[:, 0:w], sb_qk[rr, j % 2, 1, kb * P:kb * P + P], sb_qk[rr, j % 2, 0, qs],
                          start=True, stop=False, skip_group_check=True)
                pe.matmul(bk[:, 0:P], cb[:, B_ID:B_ID + P], cb[:, B_STRICT:B_STRICT + P],
                          start=False, stop=True, skip_group_check=True).then_inc(b["z"], 1)

            def cum(n, i):
                u = n % 8
                kb, w, e = geometry(u)
                bk = ps[2 + u % 4]
                pe.wait_ge(b["sp"], n + 1 + 16 * i)
                for kb2 in range(kb, NB):
                    w2 = T - P * kb2
                    off = (0, 128, 384, 768)[3 - kb2]
                    tri = cf[:, C_TRI:C_TRI + P] if kb2 == kb else cf[:, C_NEG:C_NEG + P]
                    mm = pe.matmul(bk[:, w - w2:w], tri, sb_sp[:, e, off:off + w2], start=False, stop=(kb2 == NB - 1),
                                   skip_group_check=True)
                mm.then_inc(b["cum"], 1)

            def pv(n, i):
                u = n % 8
                j = n // 8
                kb, w, e = geometry(u)
                pe.wait_ge(b["w"], n + 1 + 16 * i)
                if u % 8 == 0 and not (isinstance(i, int) and j < 2):
                    pe.wait_ge(b["ev"], j + 2 * i)
                pe.matmul(ps[6 + j % 2][64 * e:64 * e + 64, kb * P:T], sb_v[:, j % 2, kb, 64 * e:64 * e + 64],
                          sb_w[:, u % 2, 0:w], start=(kb == 3), stop=(kb == 0), skip_group_check=True)\
                    .then_inc(b["pv"], 1)

            parts = [(c, k) for c in range(2) for k in range(KD)]
            share = [6, 5, 5]

            def pair(j, i, first, last):
                t = t0 + 4 + j
                rest = list(parts)
                for u in range(8):
                    z(u, j, i)
                    if not last:
                        if u == 0:
                            qk_ready(t + 1, i)
                        if u < len(share):
                            for _ in range(share[u]):
                                qk_part(t + 1, i, *rest.pop(0))
                    if not (first and u < 2):
                        cum(8 * j + u - 2, i)
                    if not (first and u < 3):
                        pv(8 * j + u - 3, i)
                    if u == 4 and not last:
                        sums(j + 1, i)

            pair(0, 0, True, False)
            with pe.Fori(0, 3) as i:
                pair(1, i, False, False)
                pair(2, i, False, False)
            pair(7, 0, False, True)
            cum(62, 0)
            pv(61, 0)
            cum(63, 0)
            pv(62, 0)
            pv(63, 0)
            def gate_step(t, i, k):
                if isinstance(i, int) and k == 0:
                    pe.wait_ge(proj_free, 2 * t)
                in_tile(t, i)
            walk(pe, t0 + 12, 4, gate_step)
            out_steps(l, t0 + 16, 4, 2)

        def shortconv(l):
            t0 = tile_base[l]
            first_tiles(l, t0, [(t0, 0, 1), (t0, 1, 1), (t0 + 1, 0, 1), (t0 + 1, 1, 1)])
            with pe.Fori(0, 15) as i:
                in_tile(t0 + 2, i)
                in_tile(t0 + 3, i)
            out_steps(l, t0 + 32, 8, 1)

        for n in PE_AHEAD:
            pe.sem_inc(s[n], 1)
        pe.wait_ge(loaded, 48)
        sum_x(0)
        for l, kind in enumerate(layers):
            (deltanet, stickbreak, shortconv)[kind](l)

    block.__exit__(None, None, None)


def constants():
    import numpy as np
    i, j = np.arange(P)[:, None], np.arange(P)[None, :]
    f = np.zeros((P, NCF), np.float32)
    f[:, C_ID:C_ID + P] = i == j
    f[:, C_ONES:C_ONES + P] = 1
    f[:, C_BLOCK:C_BLOCK + P] = i // 64 == j // 64
    f[:, C_TRI:C_TRI + P] = -1.0 * (i >= j)
    f[:, C_NEG:C_NEG + P] = -1
    for h in range(HEADS):
        f[:, C_SELK + 8 * h + h] = 1
    g = np.zeros((P, NCB), np.float32)
    g[:, B_ID:B_ID + P] = i == j
    g[:, B_SUB:B_SUB + P] = -1.0 * ((i % 2 == 0) & (j == i + 1))
    g[:, B_STRICT:B_STRICT + P] = -1e30 * (i >= j)
    g[:, B_INCL:B_INCL + P] = -1e30 * (i > j)
    for lv in range(LEVELS - 1):
        w = 2 << lv
        g[:, B_LEVEL + lv * P:B_LEVEL + lv * P + P] = (i // w % 2 == 1) & (j // w == i // w - 1)
    for h in range(HEADS):
        g[:, B_SEL + h * P:B_SEL + h * P + P] = (i % 32 == h) & (i < 3 * 32)
    return f, g.astype(mybir.dt.np(BF16))


def by_tiles(w, chunks):
    import numpy as np
    k = w.shape[0] // P
    w = w.reshape(k, P, w.shape[1])
    return [np.ascontiguousarray(w[:, :, c].transpose(1, 0, 2)).reshape(P, WT) for c in chunks]


def lay_out(layers, inp):
    import numpy as np
    cols, n = param_columns(layers)
    par = np.zeros((P, n), np.float32)
    tiles = []
    seen = {DN: 0, SB: 0, SC: 0}
    ar = np.arange
    for l, kind in enumerate(layers):
        c, j = cols[l], seen[kind]
        seen[kind] += 1
        par[:, c["norm"]:c["norm"] + KD] = inp["norm_g"][l].reshape(KD, P).T
        if kind == DN:
            w, wo = inp["dn_w_in"][j], inp["dn_w_out"][j]
            ab = np.zeros((D, 2 * P), np.float32)
            ab[:, 0:8], ab[:, 32:40] = w[:, 6144:6152], w[:, 6152:6160]
            tiles += by_tiles(ab, [ar(2 * P)])
            tiles += by_tiles(w, [ar(m * 2 * P, (m + 1) * 2 * P) for m in range(24)])
            tiles += by_tiles(wo, [ar(m * P, (m + 1) * P) for m in range(8)])
            cw = inp["dn_conv_w"][j]
            par[:, c["conv"]:c["conv"] + 128] = cw.reshape(4, 32, P).transpose(2, 1, 0).reshape(P, 128)
            par[0:8, c["dt"]] = inp["dn_dt_bias"][j]
            par[0:8, c["alog"]] = inp["dn_a_log"][j]
            par[:, c["onorm"]:c["onorm"] + 2] = inp["dn_o_norm_g"][j].reshape(2, P).T
        elif kind == SB:
            w, wo = inp["sb_w_in"][j], inp["sb_w_out"][j]
            tiles += by_tiles(w, [2 * D + ar(m * 2 * P, (m + 1) * 2 * P) for m in range(4)])
            tiles += by_tiles(w, [np.concatenate([ar(m * P, (m + 1) * P), D + ar(m * P, (m + 1) * P)]) for m in range(8)])
            tiles += by_tiles(w, [3 * D + ar(m * 2 * P, (m + 1) * 2 * P) for m in range(4)])
            tiles += by_tiles(wo, [ar(m * 2 * P, (m + 1) * 2 * P) for m in range(4)])
            par[:, c["q"]] = np.tile(inp["sb_q_norm_g"][j], 2)
            par[:, c["k"]] = np.tile(inp["sb_k_norm_g"][j], 2)
        else:
            w, wo = inp["sc_w_in"][j], inp["sc_w_out"][j]
            for m in range(16):
                ch = [q * 2 * D + ar(m * P, (m + 1) * P) for q in range(4)]
                tiles += by_tiles(w, [np.concatenate([ch[1], ch[2]]), np.concatenate([ch[0], ch[3]])])
            tiles += by_tiles(wo, [ar(m * P, (m + 1) * P) for m in range(8)])
            par[:, c["conv"]:c["conv"] + 48] = inp["sc_conv_w"][j].reshape(3, 16, P).transpose(2, 1, 0).reshape(P, 48)
    return np.stack(tiles), par


def arrays_of(layers, inp):
    import numpy as np
    tiles, par = lay_out(layers, inp)
    f, g = constants()
    x = np.ascontiguousarray(inp["x"][0].T.reshape(KD, P, T).transpose(1, 0, 2))
    return {"x_t": x, "w_tiles": tiles, "params": par, "const_f": f, "const_b": g}


def build(nc, layers, arrays):
    import numpy as np
    args = [nc.dram_tensor(n, a.shape, mybir.dt.from_np(a.dtype), kind="ExternalInput").ap() for n, a in arrays.items()]
    out = nc.dram_tensor("out_t", (P, KD, T), F32, kind="ExternalOutput").ap()
    trunk(nc, layers, *args, out)


def kernel(**inputs):
    import numpy as np
    import concourse.bacc as bacc
    from concourse.bass_utils import run_bass_kernel_spmd as run

    layers = [DN, SB, SC, DN]
    inp = {k: np.asarray(v) for k, v in inputs.items()}
    arrays = arrays_of(layers, inp)
    nc = bacc.Bacc("TRN2", target_bir_lowering=False, num_devices=1, dynamic_dma_scratch_size=1024)
    build(nc, layers, arrays)
    r = run(nc, [arrays], core_ids=[0])
    got = r.results[0]["out_t"]
    return np.ascontiguousarray(got.transpose(1, 0, 2).reshape(D, T).T).reshape(1, T, D)
```

```python
from concourse import mybir
import concourse.bass as bass

F32 = mybir.dt.float32
F32R = mybir.dt.float32r
BF16 = mybir.dt.bfloat16
ALU = mybir.AluOpType
ACT = mybir.ActivationFunctionType

P = 128
T = 512
D = 1024
KD = D // P
NB = T // P
EPS = 1e-6

HEADS = 8
GR = 4
NG = HEADS // GR
LEVELS = 7
SB_PAIRS = 8

WT = 2048

DN, SB, SC = 0, 1, 2
TILES = {DN: 1 + 16 + 8 + 8, SB: 4 + 8 + 4 + 4, SC: 32 + 8}

C_ID, C_ONES, C_BLOCK, C_TRI, C_NEG, C_SELK = 0, 128, 256, 384, 512, 640
NCF = C_SELK + 64
B_ID, B_STRICT, B_INCL, B_LEVEL = 0, 128, 256, 384
B_SEL = B_LEVEL + (LEVELS - 1) * P
B_SUB = B_SEL + HEADS * P
NCB = B_SUB + P


def param_columns(layers):
    at, cols = 0, []
    for kind in layers:
        c = {"norm": at}
        at += KD
        if kind == DN:
            c |= {"conv": at, "dt": at + 128, "alog": at + 129, "onorm": at + 130}
            at += 132
        elif kind == SB:
            c |= {"q": at, "k": at + 1}
            at += 2
        else:
            c |= {"conv": at}
            at += 48
        cols.append(c)
    return cols, at


def y_at(c):
    return (c + 8) % 16


def walk(eng, first, n, step):
    step(first, 0, 0)
    step(first + 1, 0, 1)
    if n > 4:
        with eng.Fori(0, (n - 4) // 2) as i:
            step(first + 2, i, 2)
            step(first + 3, i, 3)
    step(first + n - 2, 0, n - 2)
    step(first + n - 1, 0, n - 1)


def trunk(nc, layers, x_in, tiles, params, const_f, const_b, out):
    cols, n_params = param_columns(layers)
    n_tiles = sum(TILES[k] for k in layers)
    tile_base = [sum(TILES[k] for k in layers[:l]) for l in range(len(layers))]
    nth = [layers[:l].count(k) for l, k in enumerate(layers)]

    at = [1152]

    def sb(name, shape, dt=F32, offset=None):
        size = 2 if dt == BF16 else 4
        for s in shape[1:]:
            size *= s
        if offset is None:
            offset = at[0]
            at[0] += (size + 31) // 32 * 32
        return nc.alloc_sbuf_tensor_at(name, shape, dt, offset=offset)

    x = sb("x", [P, KD, T])
    h_hi = sb("h_hi", [P, KD, T], F32R)
    h_lo = sb("h_lo", [P, KD, T], F32R)
    w_raw = sb("w_raw", [P, 2, WT])
    w_hi = sb("w_hi", [P, 2, WT], F32R)
    w_lo = sb("w_lo", [P, 2, WT], F32R)
    big_at = at[0]
    big = sb("big", [P, 32, T])
    y_hi = sb("y_hi", [P, 16, T], F32R, offset=big_at)
    y_lo = sb("y_lo", [P, 16, T], F32R, offset=big_at + 16 * T * 4)
    v_tok = sb("v_tok", [P, NB, D], offset=big_at)
    o_sb = sb("o_sb", [P, SB_PAIRS, T], offset=big_at + 24 * T * 4)

    sp_hi = sb("sp_hi", [P, 2, 1152], F32R, offset=big_at + 8 * T * 4)
    sp_lo = sb("sp_lo", [P, 2, 1152], F32R, offset=big_at + (8 * T + 2304) * 4)
    tri_r = sb("tri_r", [P, 2 * P], F32R, offset=big_at + (8 * T + 4608) * 4)

    arena = at[0]
    at[0] += 48 * 1024

    def in_arena(name, word, shape, dt=F32):
        return sb(name, shape, dt, offset=arena + 4 * word)

    cf = sb("cf", [P, NCF])
    cb = sb("cb", [P, NCB], BF16)
    par = sb("par", [P, n_params])
    rows = sb("rows", [P, T])
    row_parts = sb("row_parts", [P, 3, T], BF16)
    rows_b = sb("rows_b", [P, P])
    tok = sb("tok", [P, P])
    bexp = sb("bexp", [P, HEADS])
    g_end = sb("g_end", [P, HEADS])
    tok_neg = sb("tok_neg", [P, HEADS])
    gq8 = sb("gq8", [P, 1])
    assert at[0] <= nc.sbuf_usable_end, (at[0], nc.sbuf_usable_end)

    ident = cf[:, C_ID:C_ID + P]
    ones = cf[:, C_ONES:C_ONES + P]

    sq = in_arena("sq", 0, [P, 2, T])
    rstd = in_arena("rstd", 1024, [P, T])
    hf = in_arena("hf", 1536, [P, 2, T])
    acc = in_arena("acc", 2560, [P, 4, T])
    sp_a = in_arena("sp_a", 4608, [P, T])
    sp_b = in_arena("sp_b", 5120, [P, T])
    sp_c = in_arena("sp_c", 5632, [P, T])
    gate = in_arena("gate", 6144, [P, 4, T])
    yf = in_arena("yf", 8192, [P, 4, T])
    nsq = in_arena("nsq", 10240, [P, 3, T])
    nr = in_arena("nr", 11776, [P, T])
    mid = in_arena("mid", 8192, [P, T], BF16)
    ab_s = in_arena("ab_s", 7680, [P, T])
    ksq = in_arena("ksq", 6144, [P, 2, T])
    rk_ln = in_arena("rk_ln", 7168, [P, T])
    kn = in_arena("kn", 0, [P, HEADS, P])
    attn_t = in_arena("attn_t", 1024, [P, HEADS, P])
    inv_t = in_arena("inv_t", 2048, [P, HEADS, P])
    q_dec = in_arena("q_dec", 3072, [P, HEADS, P])
    decay = in_arena("decay", 4096, [P, HEADS, P])
    inv = in_arena("inv", 5120, [P, HEADS, P])
    l_t = in_arena("l_t", 6144, [P, HEADS, P])
    prod = in_arena("prod", 7168, [P, HEADS, P])
    vb = in_arena("vb", 8192, [P, HEADS, 2 * P])
    state = in_arena("state", 10240, [P, HEADS, 2 * P])
    k_beta = inv
    k_in = inv
    k_out = l_t
    w_neg = prod
    sb_sp = in_arena("sb_sp", 0, [P, 2, 1280])
    sb_w = in_arena("sb_w", 2560, [P, 2, T])
    sb_t = in_arena("sb_t", 3584, [P, 2, T])
    sb_sq = in_arena("sb_sq", 4608, [P, 2, T])
    sb_raw = in_arena("sb_raw", 5632, [P, 2, T])
    sb_r = in_arena("sb_r", 6656, [P, 2, T])
    sb_qk = in_arena("sb_qk", 7680, [P, 2, 2, T])
    sb_v = in_arena("sb_v", 9728, [P, 2, NB, P])
    sc_c = in_arena("sc_c", 2560, [P, T])
    sc_cu = in_arena("sc_cu", 3072, [P, T + 2])
    sc_acc = in_arena("sc_acc", 3600, [P, T])
    sc_y = in_arena("sc_y", 4112, [P, T])
    sc_gate = in_arena("sc_gate", 4624, [P, T])
    sc_yf = in_arena("sc_yf", 5136, [P, T])

    ps = [nc.alloc_psum_tensor(f"ps{i}", [P, T], F32) for i in range(8)]

    def bank(s, c):
        return ps[2 * (s % 2) + c]

    def sem(name):
        return nc.alloc_semaphore(name)

    par_loaded, loaded = sem("params_loaded"), sem("const_loaded")
    x_loaded = [sem(f"x_loaded{m}") for m in range(KD // 2)]
    raw = [sem("raw0_loaded"), sem("raw1_loaded")]
    hi_done, lo_done = sem("w_hi_done"), sem("w_lo_done")
    proj_done, proj_free = sem("proj_done"), sem("proj_free")
    stored = sem("stored")
    sq_done, sum_done = sem("x_sq_done"), sem("x_sum_done")
    ss_done = sem("x_ss_done")
    x_done = sem("x_done")
    ln_done, rstd_done = sem("ln_done"), sem("rstd_done")
    hf_done, hhi_done, h_done = sem("hf_done"), sem("hhi_done"), sem("h_done")
    first_done = sem("first_tiles_done")
    first_used = sem("x_gain_used")
    ab_done, turned_rstd, rstd_tok = sem("ab_scaled"), sem("rstd_turned"), sem("rstd_by_token")
    yf_done, yhi_done, y_done = sem("yf_done"), sem("yhi_done"), sem("y_done")
    dn_a, dn_v = sem("dn_rows_act"), sem("dn_rows_dve")
    zeroed = sem("rows_zeroed")
    conv_step, conv_done, silu_done = sem("conv_step"), sem("conv_done"), sem("silu_done")
    part_step, parts_done = sem("row_part_step"), sem("row_parts_done")
    ksq_done, kss_done = sem("ksq_done"), sem("kss_done")
    names = ("rkbc bbc gmask gbc2 tokt vt ktok kk qk xt turned pm du wt vn ot0 ot su "
             "kn kbeta tok tokneg gend bexp vb lt at u0 u0i pe_p ue kin kout sst "
             "rows_b vstage eg dec tokexp x0 xe wneg vne oe rk vstage2 qdec").split()
    s = {n: sem("dn_" + n) for n in names}
    PE_AHEAD, ACT_AHEAD = ("tokt", "wt", "vn", "ot", "su"), ("wneg", "vne", "oe")
    nsum_done = sem("o_sq_summed")
    nsq_done, nss_done, nln_done, nr_done, on_done, gate_done = (
        sem(n) for n in ("o_sq_done", "o_ss_done", "o_ln_done", "o_rstd_done", "o_norm_done", "gate_done"))
    b = {n: sem("sb_" + n) for n in
         "gq8 tri raw sq ss r qk v z abs exp ln1 sp sph spl cum w pv ev gate".split()}
    c_ = {n: sem("sc_" + n) for n in "zero c cu cstep conv y gate".split()}

    dn_gate0 = [tile_base[l] + 17 for l in range(len(layers))]
    y_base = []
    n_y = 0
    for kind in layers:
        y_base.append(n_y)
        n_y += 8 if kind == SB else 16

    block = nc.Block()
    blk = block.__enter__()

    @blk.sync
    def _(sp):
        sp.dma_start(par[:, :], params).then_inc(par_loaded, 16)
        for m in range(KD // 2):
            sp.dma_start(x[:, 2 * m:2 * m + 2, :], x_in[:, 2 * m:2 * m + 2, :]).then_inc(x_loaded[m], 16)
            if m == 0:
                sp.dma_start(w_raw[:, 0, :], tiles[0]).then_inc(raw[0], 16)
        sp.dma_start(cf[:, :], const_f).then_inc(loaded, 16)
        sp.dma_start(w_raw[:, 1, :], tiles[1]).then_inc(raw[1], 16)
        sp.dma_start(cb[:, :], const_b).then_inc(loaded, 16)
        pairs = n_tiles // 2
        with sp.Fori(1, pairs) as i:
            for t in range(2):
                sp.wait_ge(lo_done, 2 * i + t - 1)
                sp.dma_start(w_raw[:, t, :], tiles[2 * i + t]).then_inc(raw[t], 16)
        if n_tiles % 2:
            sp.wait_ge(lo_done, n_tiles - 2)
            sp.dma_start(w_raw[:, 0, :], tiles[n_tiles - 1]).then_inc(raw[0], 16)
        for m in range(KD):
            sp.wait_ge(x_done, KD * (len(layers) - 1) + m + 1)
            sp.dma_start(out[:, m, :], x[:, m, :]).then_inc(stored, 16)
        sp.wait_ge(stored, 16 * KD)

    @blk.gpsimd
    def _(pool):
        pool.memset(rows[:, :], 0.0).then_inc(zeroed, 1)
        pool.memset(row_parts[:, :, :], 0.0).then_inc(zeroed, 1)

        def low(t, i, slot):
            pool.wait_ge(hi_done, 2 * i + t + 1)
            pool.tensor_tensor(w_lo[:, slot, :], w_raw[:, slot, :], w_hi[:, slot, :].bitcast(F32),
                               ALU.subtract).then_inc(lo_done, 1)

        def lows(first, n):
            with pool.Fori(0, n // 2) as i:
                low(first, i, first % 2)
                low(first + 1, i, (first + 1) % 2)
            if n % 2:
                low(first + n - 1, 0, (first + n - 1) % 2)

        def chunks(d):
            with pool.Fori(0, NB) as bi:
                def v(per, k):
                    return NB * d * per + bi * per + k

                pool.wait_ge(s["su"], v(4, 1))
                pool.wait_ge(silu_done, 32 * (d + 1))
                pool.tensor_copy(l_t[:, :, :], big[:, 24:32, bass.ts(bi, P)]).then_inc(s["vstage2"], 1)
                for g in range(NG):
                    pool.wait_ge(s["ot"], v(4, 1))
                    pool.wait_ge(s["eg"], v(2, g + 1))
                    gs = slice(GR * g, GR * g + GR)
                    pool.tensor_tensor(q_dec[:, gs, :], decay[:, gs, :], big[:, gs, bass.ts(bi, P)], ALU.mult)\
                        .then_inc(s["qdec"], 1)

        for l, kind in enumerate(layers):
            if kind == DN:
                lows(tile_base[l], 18)
                chunks(nth[l])
                lows(tile_base[l] + 18, TILES[kind] - 18)
            else:
                lows(tile_base[l], TILES[kind])

    @blk.scalar
    def _(act):
        def settle():
            act.wait_ge(par_loaded, 16)

        def exp_and_ln():
            act.preload_act_table_set("natural_log_exp_and_others")

        early = {t + j for t in tile_base for j in (2, 3)}

        def hi(t, i=0, freed=None):
            if t >= n_tiles or (freed is None and isinstance(i, int) and t in early):
                return
            act.wait_ge(raw[t % 2], 16 * (t // 2 + 1) + 16 * i)
            if freed is not None:
                act.wait_ge(first_done, freed)
            elif t >= 2:
                act.wait_ge(proj_done, 2 * (t - 1) + 4 * i)
            act.activation(w_hi[:, t % 2, :], w_raw[:, t % 2, :], ACT.Copy).then_inc(hi_done, 1)

        def round_x(l, m, i=0, per=1):
            act.wait_ge(hf_done, 2 * KD * l + m + 1 + 2 * per * i)
            settle()
            act.activation(h_hi[:, m + 2 * per * i, :], hf[:, m % 2, :], ACT.Copy).then_inc(hhi_done, 1)

        def square_x(l, m, i=0, per=1):
            n = KD * l + m + 2 * per * i
            if l:
                act.wait_ge(x_done, n - KD + 1)
            if isinstance(i, int) and m < 2:
                if l:
                    act.wait_ge(ss_done, l)
            else:
                act.wait_ge(sum_done, n - l - 1)
            settle()
            act.activation(sq[:, m % 2, :], x[:, m + 2 * per * i, :], ACT.Square).then_inc(sq_done, 1)

        def copy_c(t, i, j):
            act.wait_ge(proj_done, 2 * t + 1 + 4 * i)
            if not (isinstance(i, int) and j == 0):
                act.wait_ge(c_["cu"], j + i)
            act.activation(sc_c[:, :], bank(t, 0)[:, :], ACT.Copy).then_inc(c_["c"], 1)

        def norm(l):
            t0 = tile_base[l]
            hi(t0 + 1)
            exp_and_ln()
            act.wait_ge(ss_done, l + 1)
            act.activation(rstd[:, :], ps[7][:, :], ACT.Ln, scale=1.0 / D, bias=EPS).then_inc(ln_done, 1)
            act.wait_ge(ln_done, l + 1)
            act.activation(rstd[:, :], rstd[:, :], ACT.Exp, scale=-0.5).then_inc(rstd_done, 1)
            hi(t0 + 2, freed=4 * l + 2)
            for k in range(KD):
                if k == 2 and layers[l] == SC:
                    copy_c(t0, 0, 0)
                if k < KD - 1:
                    act.wait_ge(first_used, (KD - 1) * l + k + 1)
                else:
                    act.wait_ge(first_done, 4 * l + 4)
                act.wait_ge(hf_done, 2 * KD * l + KD + k + 1)
                act.activation(h_hi[:, k, :], hf[:, k % 2, :], ACT.Copy).then_inc(hhi_done, 1)
            hi(t0 + 3, freed=4 * l + 4)

        def out_steps(l, first, n, per):
            def step(t, i, k):
                hi(t + 1, i)
                if l + 1 < len(layers):
                    for c in range(per):
                        round_x(l + 1, per * k + c, i, per)
                        square_x(l + 1, per * k + c, i, per)

            walk(act, first, n, step)

        def deltanet(l):
            d, t0, c0 = nth[l], tile_base[l], cols[l]
            a0 = 6 * d
            act.wait_ge(ab_done, d + 1)
            act.activation(sp_a[0:8, :], ab_s[0:8, :], ACT.Abs, bias=par[0:8, c0["dt"]:c0["dt"] + 1]).then_inc(dn_a, 1)
            act.wait_ge(dn_a, a0 + 1)
            act.activation(sp_a[0:8, :], sp_a[0:8, :], ACT.Exp, scale=-1.0).then_inc(dn_a, 1)
            act.wait_ge(dn_a, a0 + 2)
            act.activation(sp_a[0:8, :], sp_a[0:8, :], ACT.Ln, bias=1.0).then_inc(dn_a, 1)
            act.activation(sp_c[32:40, :], ab_s[32:40, :], ACT.Exp, scale=-1.0).then_inc(dn_a, 1)
            act.activation(bexp[0:8, 0:1], par[0:8, c0["alog"]:c0["alog"] + 1], ACT.Exp).then_inc(dn_a, 1)

            def silu(k, i=0):
                for c in range(2):
                    act.wait_ge(conv_done, 32 * d + 2 * k + c + 1 + 4 * i)
                    settle()
                    act.activation(big[:, 2 * k + c + 4 * i, :], acc[:, 2 * (k % 2) + c, :], ACT.Silu)\
                        .then_inc(silu_done, 1)

            def step(t, i, k):
                hi(t + 1, i)
                if not (isinstance(i, int) and k == 0):
                    silu(k - 1, i)

            walk(act, t0 + 1, 8, step)
            for k in range(8, 8 + HEADS // 2):
                step(t0 + 1 + k, 0, k)
                for h in (2 * k - 16, 2 * k - 15):
                    act.wait_ge(silu_done, 32 * d + 9 + h)
                    if h >= 2:
                        act.wait_ge(kss_done, HEADS * d + h - 1)
                    act.activation(ksq[:, h % 2, :], big[:, HEADS + h, :], ACT.Square).then_inc(ksq_done, 1)
            step(t0 + 13, 0, 12)
            exp_and_ln()
            act.wait_ge(dn_v, 9 * d + 9)
            act.activation(rows[96:104, :], sp_b[0:8, :], ACT.Exp).then_inc(dn_a, 1)
            act.wait_ge(kss_done, HEADS * (d + 1))
            act.activation(rk_ln[0:8, :], ps[7][0:8, :], ACT.Ln, bias=EPS).then_inc(s["rk"], 1)
            act.wait_ge(s["rk"], 2 * d + 1)
            act.activation(rows[64:72, :], rk_ln[0:8, :], ACT.Exp, scale=-0.5).then_inc(s["rk"], 1)
            for k in range(13, 16):
                step(t0 + 1 + k, 0, k)
            silu(15)
            exp_and_ln()
            act.wait_ge(s["rk"], 2 * d + 2)

            with act.Fori(0, NB) as bi:
                def v(per, k):
                    return NB * d * per + bi * per + k

                act.wait_ge(dn_a, a0 + 6)
                act.wait_ge(s["gend"], NB * d + d + 1 + bi)
                act.wait_ge(s["tokt"], v(1, 1))
                settle()
                act.activation(rows_b[:, :], rows[:, bass.ts(bi, P)], ACT.Copy).then_inc(s["rows_b"], 1)
                act.wait_ge(s["vn"], v(4, 1))
                act.wait_ge(silu_done, 32 * (d + 1))
                settle()
                act.activation(prod[:, :, :], big[:, 16:24, bass.ts(bi, P)], ACT.Copy).then_inc(s["vstage"], 1)
                act.wait_ge(s["ot"], v(4, 1))
                act.wait_ge(s["tokneg"], v(1, 1))
                for h in range(HEADS):
                    if h % GR == 0:
                        act.wait_ge(s["gmask"], v(2, h // GR + 1))
                    act.activation(attn_t[:, h, :], ps[h // GR][:, (h % GR) * P:(h % GR) * P + P], ACT.Exp,
                                   bias=tok_neg[:, h:h + 1]).then_inc(s["dec"], 1)
                act.wait_ge(s["tok"], v(1, 1))
                act.activation(bexp[:, :], tok[:, 0:8], ACT.Exp).then_inc(s["tokexp"], 1)
                for g in range(NG):
                    act.wait_ge(s["xt"], v(2, g + 1))
                    act.activation(inv[:, GR * g:GR * g + GR, :], ps[g][:, :], ACT.Copy).then_inc(s["x0"], 1)
                act.wait_ge(s["sst"], NB * d * 8 + 8 * d + 8 + bi * 8)
                for g in range(NG):
                    act.wait_ge(s["gbc2"], v(2, g + 1))
                    act.activation(decay[:, GR * g:GR * g + GR, :], ps[4 + g][:, :], ACT.Exp).then_inc(s["eg"], 1)
                n_l = LEVELS - 1
                for lv in range(n_l - 1):
                    for g in range(NG):
                        act.wait_ge(s["turned"], v(2 * (n_l - 1), 2 * lv + g + 1))
                        act.activation(inv[:, GR * g:GR * g + GR, :], ps[6 + g][:, :], ACT.Copy).then_inc(s["xe"], 1)
                for g in range(NG):
                    act.wait_ge(s["wt"], v(2, g + 2))
                    act.activation(w_neg[:, GR * g:GR * g + GR, :], ps[2 + g][:, :], ACT.Copy, scale=-1.0)\
                        .then_inc(s["wneg"], 1)

                def o_out(p):
                    act.wait_ge(s["ot"], v(4, p + 2))
                    settle()
                    act.activation(big[:, 16 + 4 * p:20 + 4 * p, bass.ds((bi + 1) * P - P, P)],
                                   ps[6 + p % 2].rearrange("p (c t) -> p c t", t=P), ACT.Copy)\
                        .then_inc(s["oe"], 1)

                for p in range(4):
                    act.wait_ge(s["vn"], v(4, p + 2))
                    act.activation(vb[:, 2 * p:2 * p + 2, :], ps[4 + p % 2][:, :], ACT.Copy)\
                        .then_inc(s["vne"], 1)
                    if p:
                        o_out(p - 1)
                o_out(3)

            g0 = dn_gate0[l]
            kq = (EPS * P * 2 * P) ** 0.5

            def squares(h, i=0):
                n = HEADS * d + h + 2 * i
                if not (isinstance(i, int) and h == 0):
                    act.wait_ge(nss_done, n)
                else:
                    act.wait_ge(s["oe"], NB * 4 * (d + 1) + 1)
                    act.wait_ge(s["sst"], (NB + 1) * 8 * (d + 1))
                for c in range(2):
                    act.activation(nsq[:, c, :], big[:, 16 + 2 * h + c + 4 * i, :], ACT.Square).then_inc(nsq_done, 1)
                act.activation(nsq[:, 2, :], big[:, h + 2 * i, :], ACT.Square, scale=kq).then_inc(nsq_done, 1)

            def o_rstd(h, i=0):
                n = HEADS * d + h + 2 * i
                exp_and_ln()
                act.wait_ge(nss_done, n + 1)
                if not (isinstance(i, int) and h == 0):
                    act.wait_ge(on_done, 2 * n)
                act.activation(nr[:, :], ps[4][:, :], ACT.Ln, scale=1.0 / (2 * P), bias=EPS * P * EPS).then_inc(nln_done, 1)
                act.wait_ge(nln_done, n + 1)
                act.activation(nr[:, :], nr[:, :], ACT.Exp, scale=-0.5).then_inc(nr_done, 1)

            def gates(t, h, i=0):
                for c in range(2):
                    act.wait_ge(proj_done, 2 * t + c + 1 + 4 * i)
                    if not (isinstance(i, int) and h < 2):
                        act.wait_ge(yf_done, y_base[l] + 2 * h - 4 + c + 1 + 4 * i)
                    act.activation(gate[:, 2 * (h % 2) + c, :], bank(t, c)[:, :], ACT.Silu).then_inc(gate_done, 1)

            def y_his(h, i=0):
                for c in range(2):
                    k = 2 * h + c
                    act.wait_ge(yf_done, y_base[l] + k + 1 + 4 * i)
                    if isinstance(i, int):
                        dst = y_hi[:, y_at(k), :]
                    else:
                        dst = y_hi[:, k + 4 * i, :]
                    act.activation(dst, yf[:, 2 * (h % 2) + c, :], ACT.Copy).then_inc(yhi_done, 1)

            squares(0)
            for h in range(HEADS):
                t = g0 + h
                o_rstd(h)
                if h + 1 < HEADS:
                    squares(h + 1)
                hi(t + 1)
                if h:
                    if h == 1:
                        act.wait_ge(nsq_done, 3 * (HEADS * d + 2))
                    act.wait_ge(nsq_done, 3 * (HEADS * d + min(h + 2, HEADS)))
                    y_his(h - 1)
                gates(t, h)
            y_his(HEADS - 1)
            out_steps(l, g0 + 8, 8, 1)

        def stickbreak(l):
            n0, t0 = nth[l], tile_base[l]
            assert n0 == 0

            def v_step(t, i, k):
                if k or not isinstance(i, int):
                    hi(t + 1, i)
                if k < 2:
                    return
                for c in range(2):
                    act.wait_ge(proj_done, 2 * t + c + 1 + 4 * i)
                    w = 2 * P
                    settle()
                    act.activation(v_tok[:, 2 * c:2 * c + 2, bass.ds(w * k + 2 * w * i, w)],
                                   bank(t, c).rearrange("p (b n) -> p b n", b=2), ACT.Copy)\
                        .then_inc(proj_free, 1)

            walk(act, t0, 4, v_step)

            def square_qk(t, j, i=0):
                for c in range(2):
                    act.wait_ge(b["raw"], 2 * j + c + 1 + 4 * i)
                    if not (isinstance(i, int) and j == 0):
                        act.wait_ge(b["ss"], 2 * j - 1 + c + 4 * i)
                    act.activation(sb_sq[:, c, :], sb_raw[:, c, :], ACT.Square).then_inc(b["sq"], 1)

            def rms_qk(j, i=0):
                for c in range(2):
                    act.wait_ge(b["ss"], 2 * j + c + 1 + 4 * i)
                    if not (isinstance(i, int) and j == 0):
                        act.wait_ge(b["qk"], 2 * j - 1 + c + 4 * i)
                    act.activation(sb_r[:, c, :], ps[c][:, :], ACT.Ln, scale=1.0 / 64, bias=EPS).then_inc(proj_free, 1)
                    act.wait_ge(proj_free, 2 * (t0 + 4 + j) + c + 1 + 4 * i)
                    act.activation(sb_r[:, c, :], sb_r[:, c, :], ACT.Exp, scale=-0.5).then_inc(b["r"], 1)

            def softplus(u, j, i):
                n = 8 * j + u
                kb = 3 - u % 4
                w = T - P * kb
                zb, tt = ps[2 + u % 4][:, 0:w], sb_t[:, u % 2, 0:w]
                act.wait_ge(b["z"], n + 1 + 16 * i)
                if not (isinstance(i, int) and n < 2):
                    act.wait_ge(b["sp"], n - 1 + 16 * i)
                act.activation(tt, zb, ACT.Abs).then_inc(b["abs"], 1)
                act.wait_ge(b["abs"], n + 1 + 16 * i)
                act.activation(tt, tt, ACT.Exp, scale=-1.0).then_inc(b["exp"], 1)
                act.wait_ge(b["exp"], n + 1 + 16 * i)
                act.activation(tt, tt, ACT.Ln, bias=1.0).then_inc(b["ln1"], 1)

            def weights(n, i):
                u = n % 8
                kb = 3 - u % 4
                w = T - P * kb
                act.wait_ge(b["cum"], n + 1 + 16 * i)
                if not (isinstance(i, int) and n < 2):
                    act.wait_ge(b["pv"], n - 1 + 16 * i)
                act.activation(sb_w[:, u % 2, 0:w], ps[2 + u % 4][:, 0:w], ACT.Exp).then_inc(b["w"], 1)

            hi(t0 + 5)
            square_qk(t0 + 4, 0)
            rms_qk(0)

            def pair(j, i, first, last):
                t = t0 + 4 + j
                hi(t + 2, i)
                for u in range(8):
                    softplus(u, j, i)
                    if not (first and u < 2):
                        weights(8 * j + u - 2, i)
                    if u == 4 and not last:
                        square_qk(t + 1, j + 1, i)
                    if u == 5 and not last:
                        rms_qk(j + 1, i)

            pair(0, 0, True, False)
            with act.Fori(0, 3) as i:
                pair(1, i, False, False)
                pair(2, i, False, False)
            pair(7, 0, False, True)
            weights(62, 0)
            weights(63, 0)

            def y_his(k, i=0):
                for c in range(2):
                    n = 2 * k + c
                    act.wait_ge(yf_done, y_base[l] + n + 1 + 4 * i)
                    settle()
                    act.activation(y_hi[:, 8 + n + 4 * i, :], yf[:, 2 * (k % 2) + c, :], ACT.Copy).then_inc(yhi_done, 1)

            def gate_step(t, i, k):
                if not (isinstance(i, int) and k == 0):
                    hi(t + 1, i)
                for c in range(2):
                    act.wait_ge(proj_done, 2 * t + c + 1 + 4 * i)
                    if not (isinstance(i, int) and k < 2):
                        act.wait_ge(yf_done, y_base[l] + 2 * k - 4 + c + 1 + 4 * i)
                    act.activation(gate[:, 2 * (k % 2) + c, :], bank(t, c)[:, :], ACT.Silu).then_inc(b["gate"], 1)
                if not (isinstance(i, int) and k == 0):
                    y_his(k - 1, i)

            walk(act, t0 + 12, 4, gate_step)
            y_his(3)
            out_steps(l, t0 + 16, 4, 2)

        def shortconv(l):
            t0 = tile_base[l]

            def y_high(k, i=0):
                act.wait_ge(yf_done, y_base[l] + k + 1 + i)
                dst = y_hi[:, y_at(k), :] if isinstance(i, int) else y_hi[:, (k + 8) % 16 + i, :]
                settle()
                act.activation(dst, sc_yf[:, :], ACT.Copy).then_inc(yhi_done, 1)

            def group(j, i, first=False):
                t = t0 + 2 * j
                if not first:
                    hi(t + 1, i)
                    y_high(j - 1, i)
                    copy_c(t, i, j)
                hi(t + 2, i)
                act.wait_ge(proj_done, 2 * t + 4 + 4 * i)
                if not first:
                    act.wait_ge(yf_done, y_base[l] + j + i)
                act.activation(sc_gate[:, :], bank(t + 1, 1)[:, :], ACT.Silu).then_inc(c_["gate"], 1)

            group(0, 0, True)
            group(1, 0)
            with act.Fori(0, 7) as i:
                group(2, i)
            with act.Fori(0, 7) as i:
                group(9, i)
            y_high(15)
            out_steps(l, t0 + 32, 8, 1)

        exp_and_ln()
        for m in range(KD):
            act.wait_ge(x_loaded[m // 2], 16)
            round_x(0, m)
            square_x(0, m)
            if m == 1:
                hi(0)
        for n in ACT_AHEAD:
            act.sem_inc(s[n], 1)
        for l, kind in enumerate(layers):
            norm(l)
            (deltanet, stickbreak, shortconv)[kind](l)

    @blk.vector
    def _(dve):
        def sum_squares(l, m, i=0, per=1):
            n = KD * l + m + 2 * per * i
            dve.wait_ge(sq_done, n + 1)
            if isinstance(i, int) and m == 0:
                if l:
                    dve.wait_ge(h_done, 2 * KD * l)
                dve.tensor_copy(rstd[:, :], sq[:, 0, :]).then_inc(sum_done, 1)
                return
            dve.wait_ge(sum_done, n - l)
            dve.tensor_tensor(rstd[:, :], rstd[:, :], sq[:, m % 2, :], ALU.add).then_inc(sum_done, 1)

        def gain_x(l, m, i=0, per=1):
            n = 2 * KD * l + m + 2 * per * i
            if not (isinstance(i, int) and m < 2):
                dve.wait_ge(h_done, n - 1)
            c0 = cols[l]["norm"]
            g = par[:, c0 + m:c0 + m + 1] if isinstance(i, int) else par[:, bass.ds(2 * per * i + (c0 + m), 1)]
            dve.tensor_scalar(hf[:, m % 2, :], x[:, m + 2 * per * i, :], g, None, ALU.mult).then_inc(hf_done, 1)

        def low_x(l, m, i=0, per=1):
            k = m + 2 * per * i
            dve.wait_ge(hhi_done, 2 * KD * l + k + 1)
            dve.tensor_tensor(h_lo[:, k, :], hf[:, m % 2, :], h_hi[:, k, :].bitcast(F32), ALU.subtract)\
                .then_inc(h_done, 1)

        def scale(l, t, c):
            dve.wait_ge(first_done, 4 * l + 2 * (t - tile_base[l]) + c + 1)
            dve.tensor_tensor(bank(t, c)[:, :], bank(t, c)[:, :], rstd[:, :], ALU.mult).then_inc(proj_done, 1)

        def scale_ab(l):
            t0, d = tile_base[l], nth[l]
            dve.wait_ge(first_done, 4 * l + 2)
            dve.tensor_tensor(ab_s[0:64, :], bank(t0, 0)[0:64, :], rstd[0:64, :], ALU.mult).then_inc(ab_done, 1)
            dve.wait_ge(ab_done, d + 1)
            dve.sem_inc(proj_done, 2)
            dve.sem_inc(proj_free, 2)

        def scale_v(l, t):
            for c in range(2):
                dve.wait_ge(first_done, 4 * l + 2 * (t - tile_base[l]) + c + 1)
                w = 2 * P * (t - tile_base[l])
                dve.tensor_tensor(v_tok[:, 2 * c:2 * c + 2, w:w + 2 * P], bank(t, c).rearrange("p (b n) -> p b n", b=2),
                                  bexp[:, 2 * c:2 * c + 2].unsqueeze(2).to_broadcast([P, 2, 2 * P]), ALU.mult)\
                    .then_inc(proj_done, 1)
                dve.wait_ge(proj_done, 2 * t + c + 1)
                dve.sem_inc(proj_free, 1)

        def times_u(t, i, j):
            dve.wait_ge(c_["c"], j + 1 + i)
            dve.wait_ge(proj_done, 2 * t + 2 + 4 * i)
            if not (isinstance(i, int) and j == 0):
                dve.wait_ge(c_["conv"], j + i)
            dve.tensor_tensor(sc_cu[:, 2:T + 2], bank(t, 1)[:, :], sc_c[:, :], ALU.mult).then_inc(c_["cu"], 1)
            dve.wait_ge(c_["cu"], j + 1 + i)
            dve.sem_inc(proj_free, 2)

        def norm(l):
            t0, kind = tile_base[l], layers[l]
            dve.wait_ge(rstd_done, l + 1)
            if kind == DN:
                scale_ab(l)
            elif kind == SC:
                scale(l, t0, 0)
                scale(l, t0, 1)

            def low(k):
                dve.wait_ge(hhi_done, 2 * KD * l + KD + k + 1)
                dve.tensor_tensor(h_lo[:, k, :], hf[:, k % 2, :], h_hi[:, k, :].bitcast(F32), ALU.subtract)\
                    .then_inc(h_done, 1)

            c0 = cols[l]["norm"]
            for k in range(KD):
                dve.wait_ge(h_done, 2 * KD * l + KD + k - 1)
                dve.scalar_tensor_tensor(hf[:, k % 2, :], x[:, k, :], par[:, c0 + k:c0 + k + 1], rstd[:, :],
                                         ALU.mult, ALU.mult).then_inc(hf_done, 1)
                if k:
                    low(k - 1)
                if k == 3 and kind == SC:
                    times_u(t0, 0, 0)
            low(KD - 1)
            if kind == SB:
                dve.wait_ge(turned_rstd, 1)
                dve.tensor_copy(bexp[:, 0:NB], ps[6][:, 0:NB]).then_inc(rstd_tok, 1)
                dve.wait_ge(rstd_tok, 1)
                scale_v(l, t0)
                scale_v(l, t0 + 1)
            else:
                scale(l, t0 + 1, 0)
                scale(l, t0 + 1, 1)

        def out_steps(l, first, n, per):
            def step(t, i, k):
                for c in range(per):
                    dve.wait_ge(proj_done, 2 * t + (c + 1 if per == 2 else 2) + 4 * i)
                    m = per * k + c
                    dve.tensor_tensor(x[:, m + 2 * per * i, :], bank(t, c)[:, :], x[:, m + 2 * per * i, :], ALU.add)\
                        .then_inc(x_done, 1)
                    dve.wait_ge(x_done, KD * l + m + 1 + 2 * per * i)
                    dve.sem_inc(proj_free, 1 if per == 2 else 2)
                    if l + 1 < len(layers):
                        gain_x(l + 1, m, i, per)
                        if not (isinstance(i, int) and m == 0):
                            low_x(l + 1, m - 1, i, per)
                            sum_squares(l + 1, m - 1, i, per)

            walk(dve, first, n, step)
            if l + 1 < len(layers):
                low_x(l + 1, KD - 1)

        def deltanet(l):
            d, t0, c0 = nth[l], tile_base[l], cols[l]
            v0, a0 = 9 * d, 6 * d

            def step(t, i, k):
                for c in range(2):
                    n = 32 * d + 2 * k + c
                    a = acc[:, 2 * (k % 2) + c, :]
                    bk = bank(t, c)

                    def w(j):
                        if isinstance(i, int):
                            at_ = c0["conv"] + 4 * (2 * k + c) + j
                            return par[:, at_:at_ + 1]
                        return par[:, bass.ds(16 * i + (c0["conv"] + 4 * (2 * k + c) + j), 1)]

                    dve.wait_ge(proj_done, 2 * t + c + 1 + 4 * i)
                    if not (isinstance(i, int) and k < 2):
                        dve.wait_ge(silu_done, n - 3 + 4 * i)
                    dve.tensor_scalar(a, bk[:, :], w(3), None, ALU.mult).then_inc(conv_step, 1)
                    for j in (1, 2):
                        dve.wait_ge(conv_step, 3 * n + j + 12 * i)
                        dve.scalar_tensor_tensor(a[:, j:T], bk[:, 0:T - j], w(3 - j), a[:, j:T], ALU.mult, ALU.add)\
                            .then_inc(conv_step, 1)
                    dve.wait_ge(conv_step, 3 * n + 3 + 12 * i)
                    dve.scalar_tensor_tensor(a[:, 3:T], bk[:, 0:T - 3], w(0), a[:, 3:T], ALU.mult, ALU.add)\
                        .then_inc(conv_done, 1)
                    dve.wait_ge(conv_done, n + 1 + 4 * i)
                    dve.sem_inc(proj_free, 1)

            def split_row(q):
                own = slice(32 * q, 32 * q + 8)
                part = [slice(32 * ((q + j) % 3), 32 * ((q + j) % 3) + 8) for j in range(3)]
                n = 12 * d + 4 * q
                dve.tensor_copy(row_parts[own, q, :], rows[own, :]).then_inc(part_step, 1)
                dve.wait_ge(part_step, n + 1)
                dve.tensor_tensor(sp_c[own, :], rows[own, :], row_parts[own, q, :], ALU.subtract).then_inc(part_step, 1)
                dve.wait_ge(part_step, n + 2)
                dve.tensor_copy(mid[own, :], sp_c[own, :]).then_inc(part_step, 1)
                dve.tensor_copy(row_parts[part[1], q, :], sp_c[own, :]).then_inc(part_step, 1)
                dve.wait_ge(part_step, n + 4)
                dve.tensor_tensor(row_parts[part[2], q, :], sp_c[own, :], mid[own, :], ALU.subtract).then_inc(parts_done, 1)

            def decay_rows():
                dve.wait_ge(dn_a, a0 + 5)
                dve.tensor_scalar(sp_b[0:8, :], ab_s[0:8, :], par[0:8, c0["dt"]:c0["dt"] + 1], 0.0, ALU.add, ALU.max)\
                    .then_inc(dn_v, 1)
                dve.wait_ge(dn_v, v0 + 1)
                dve.tensor_tensor(sp_b[0:8, :], sp_b[0:8, :], sp_a[0:8, :], ALU.add).then_inc(dn_v, 1)
                dve.wait_ge(dn_v, v0 + 2)
                dve.tensor_scalar(sp_a[0:8, :], sp_b[0:8, :], bexp[0:8, 0:1], -1.0, ALU.mult, ALU.mult).then_inc(dn_v, 1)
                dve.wait_ge(dn_v, v0 + 3)
                if d == 0:
                    dve.wait_ge(zeroed, 2)
                for n in range(NB):
                    dve.tensor_tensor_scan(rows[0:8, n * P:n * P + P], cf[0:8, C_ONES:C_ONES + P],
                                           sp_a[0:8, n * P:n * P + P], 0.0, ALU.mult, ALU.add).then_inc(dn_v, 1)
                dve.tensor_scalar(sp_c[32:40, :], sp_c[32:40, :], 1.0, None, ALU.add).then_inc(dn_v, 1)
                dve.wait_ge(dn_v, v0 + 8)
                g4 = rows[0:8, :].rearrange("p (n t) -> p n t", t=P)
                dve.tensor_tensor(sp_b[0:8, :].rearrange("p (n t) -> p n t", t=P),
                                  g4[:, :, P - 1:P].to_broadcast([8, NB, P]), g4, ALU.subtract).then_inc(dn_v, 1)

            step(t0 + 1, 0, 0)
            decay_rows()
            step(t0 + 2, 0, 1)
            dve.reciprocal(rows[32:40, :], sp_c[32:40, :]).then_inc(s["gend"], 1)
            step(t0 + 3, 0, 2)
            split_row(0)
            step(t0 + 4, 0, 3)
            dve.wait_ge(s["gend"], (NB + 1) * d + 1)
            split_row(1)
            walk(dve, t0 + 5, 8, lambda t, i, k: step(t, i, k + 4))
            step(t0 + 13, 0, 12)
            dve.wait_ge(s["rk"], 2 * d + 2)
            split_row(2)
            for k in range(13, 16):
                step(t0 + 1 + k, 0, k)
            dve.wait_ge(silu_done, 32 * d + 32)
            dve.memset(state[:, :, :], 0.0).then_inc(s["sst"], 8)

            with dve.Fori(0, NB) as bi:
                def v(per, k):
                    return NB * d * per + bi * per + k

                def gr(t, g):
                    return t[:, GR * g:GR * g + GR, :]

                def bk(n, w=P):
                    return ps[n].rearrange("p (h t) -> p h t", t=w)

                for g in range(NG):
                    dve.wait_ge(s["rkbc"], v(2, g + 1))
                    dve.wait_ge(s["wt"], v(2, 1))
                    dve.tensor_tensor(gr(kn, g), bk(2 + g), big[:, 8 + GR * g:8 + GR * g + GR, bass.ts(bi, P)], ALU.mult)\
                        .then_inc(s["kn"], 1)
                dve.wait_ge(s["tokt"], v(1, 2))
                dve.tensor_copy(tok[:, :], ps[6][:, 0:P]).then_inc(s["tok"], 1)
                for g in range(NG):
                    dve.wait_ge(s["bbc"], v(2, g + 1))
                    dve.wait_ge(s["kn"], v(2, g + 1))
                    dve.tensor_tensor(gr(k_beta, g), bk(4 + g), gr(kn, g), ALU.mult).then_inc(s["kbeta"], 1)
                    if g == 0:
                        dve.wait_ge(s["tok"], v(1, 1))
                        dve.tensor_scalar(tok_neg[:, :], tok[:, 0:8], -1.0, None, ALU.mult).then_inc(s["tokneg"], 1)

                def beta_v(p):
                    dve.wait_ge(s["vt"], v(4, p + 1))
                    dve.wait_ge(s["su"], v(4, 1))
                    bank_ = ps[(7, 6, 2, 3)[p]].rearrange("p (h t) -> p h t", t=2 * P)
                    dve.tensor_tensor(vb[:, 2 * p:2 * p + 2, :], bank_,
                                      tok[:, 32 + 2 * p:34 + 2 * p].unsqueeze(2).to_broadcast([P, 2, 2 * P]), ALU.mult)\
                        .then_inc(s["vb"], 1)

                beta_v(0)
                beta_v(1)
                for g in range(NG):
                    dve.wait_ge(s["kk"], v(2, g + 1))
                    dve.wait_ge(s["dec"], v(8, GR * g + GR))
                    dve.wait_ge(s["vt"], v(4, 4))
                    dve.tensor_tensor(gr(l_t, g), bk(4 + g), gr(attn_t, g), ALU.mult).then_inc(s["lt"], 1)
                sub = cb[:, B_SUB:B_SUB + P].unsqueeze(1).to_broadcast([P, GR, P])
                idb = ident.unsqueeze(1).to_broadcast([P, GR, P])
                for g in range(NG):
                    dve.wait_ge(s["lt"], v(2, g + 1))
                    dve.tensor_tensor(gr(inv_t, g), gr(l_t, g), sub, ALU.mult).then_inc(s["u0"], 1)
                for g in range(NG):
                    dve.wait_ge(s["u0"], v(2, g + 1))
                    dve.tensor_tensor(gr(inv_t, g), gr(inv_t, g), idb, ALU.add).then_inc(s["u0i"], 1)
                beta_v(2)
                beta_v(3)
                for g in range(NG):
                    dve.wait_ge(s["qk"], v(2, g + 1))
                    dve.tensor_tensor(gr(attn_t, g), bk(7 - g), gr(attn_t, g), ALU.mult).then_inc(s["at"], 1)
                n_l = LEVELS - 1
                for lv in range(n_l):
                    mask = cb[:, B_LEVEL + lv * P:B_LEVEL + lv * P + P].unsqueeze(1).to_broadcast([P, GR, P])
                    for g in range(NG):
                        dve.wait_ge(s["pm"], v(2 * n_l, 2 * lv + g + 1))
                        dve.tensor_tensor(gr(prod, g), bk(2 + g), mask, ALU.mult).then_inc(s["pe_p"], 1)
                    if lv == 1:
                        dve.wait_ge(s["eg"], v(2, 2))
                        dve.wait_ge(s["sst"], NB * d * 8 + 8 * d + 8 + bi * 8)
                        dve.tensor_copy(g_end[:, :], decay[:, :, P - 1]).then_inc(s["gend"], 1)
                        dve.wait_ge(s["tokexp"], v(1, 1))
                        dve.tensor_tensor(bexp[:, :], bexp[:, :], tok[:, 32:40], ALU.mult).then_inc(s["bexp"], 1)
                    for g in range(NG):
                        dve.wait_ge(s["du"], v(2 * n_l, 2 * lv + g + 1))
                        if lv:
                            dve.wait_ge(s["ue"], v(2 * n_l, 2 * lv + g - 1))
                        else:
                            dve.wait_ge(s["u0i"], v(2, g + 1))
                        dve.tensor_tensor(gr(inv_t, g), gr(inv_t, g), bk(4 + g), ALU.subtract).then_inc(s["ue"], 1)
                for g in range(NG):
                    dve.wait_ge(s["ktok"], v(2, g + 1))
                    dve.wait_ge(s["pm"], v(2 * n_l, 2 * n_l))
                    dve.wait_ge(s["bexp"], v(1, 1))
                    dve.tensor_tensor(gr(k_in, g), bk(g), bexp[:, GR * g:GR * g + GR].unsqueeze(2).to_broadcast([P, GR, P]),
                                      ALU.mult).then_inc(s["kin"], 1)
                for g in range(NG):
                    dve.tensor_tensor(gr(k_out, g), bk(g),
                                      tok[:, 96 + GR * g:96 + GR * g + GR].unsqueeze(2).to_broadcast([P, GR, P]),
                                      ALU.mult).then_inc(s["kout"], 1)
                for h in range(HEADS):
                    p = h // 2
                    if h == 0:
                        dve.wait_ge(s["gend"], NB * d + d + 2 + bi)
                    if h % 2 == 0:
                        dve.wait_ge(s["ot0"], v(4, p + 1))
                        dve.wait_ge(s["su"], v(4, p + 2))
                    dve.scalar_tensor_tensor(state[:, h, :], state[:, h, :], g_end[:, h:h + 1],
                                             ps[p % 2][:, (h % 2) * 2 * P:(h % 2 + 1) * 2 * P], ALU.mult, ALU.add)\
                        .then_inc(s["sst"], 1)

            co = c0["onorm"]

            def sum_norm(h):
                n = HEADS * d + h
                for c in (1, 2):
                    dve.wait_ge(nsq_done, 3 * n + c + 1)
                    if c == 2:
                        dve.wait_ge(nsum_done, 2 * n + 1)
                    dve.tensor_tensor(nsq[:, 0, :], nsq[:, 0, :], nsq[:, c, :], ALU.add).then_inc(nsum_done, 1)

            sum_norm(0)
            for h in range(HEADS):
                n = HEADS * d + h
                if h + 1 < HEADS:
                    sum_norm(h + 1)
                for c in range(2):
                    ob = big[:, 16 + 2 * h + c, :]
                    dve.wait_ge(nr_done, n + 1)
                    dve.scalar_tensor_tensor(ob, ob, par[:, co + c:co + c + 1], nr[:, :], ALU.mult, ALU.mult)\
                        .then_inc(on_done, 1)
                for c in range(2):
                    k = y_base[l] + 2 * h + c
                    dve.wait_ge(gate_done, 2 * n + c + 1)
                    dve.wait_ge(on_done, 2 * n + c + 1)
                    if h >= 2:
                        dve.wait_ge(y_done, k - 3)
                    slot = 2 * (h % 2) + c
                    dve.tensor_tensor(yf[:, slot, :], big[:, 16 + 2 * h + c, :], gate[:, slot, :], ALU.mult)\
                        .then_inc(yf_done, 1)
                    dve.sem_inc(proj_free, 1)
                if h:
                    y_lows2(l, h - 1)
            y_lows2(l, HEADS - 1)
            out_steps(l, dn_gate0[l] + 8, 8, 1)

        def y_lows2(l, h, i=0):
            for c in range(2):
                n = 2 * h + c
                slot = 2 * (h % 2) + c
                dve.wait_ge(yhi_done, y_base[l] + n + 1 + 4 * i)
                if isinstance(i, int):
                    hi_b, lo_b = y_hi[:, y_at(n), :], y_lo[:, n, :]
                else:
                    hi_b, lo_b = y_hi[:, 8 + n + 4 * i, :], y_lo[:, n + 4 * i, :]
                dve.tensor_tensor(lo_b, yf[:, slot, :], hi_b.bitcast(F32), ALU.subtract).then_inc(y_done, 1)

        def stickbreak(l):
            t0, c0 = tile_base[l], cols[l]
            dve.sem_inc(b["ev"], 1)
            dve.tensor_scalar(gq8[:, :], par[:, c0["q"]:c0["q"] + 1], 0.125, None, ALU.mult).then_inc(b["gq8"], 1)
            dve.tensor_copy(tri_r[:, :], cf[:, C_TRI:C_TRI + 2 * P]).then_inc(b["tri"], 1)

            def raws(t, j, i=0):
                for c in range(2):
                    dve.wait_ge(proj_done, 2 * t + c + 1 + 4 * i)
                    if not (isinstance(i, int) and j == 0):
                        dve.wait_ge(b["qk"], 2 * j - 1 + c + 4 * i)
                    dve.tensor_copy(sb_raw[:, c, :], ps[c][:, :]).then_inc(b["raw"], 1)

            def scaled(j, i=0):
                par_ = j % 2
                for c, gain in enumerate((gq8[:, 0:1], par[:, c0["k"]:c0["k"] + 1])):
                    dve.wait_ge(b["r"], 2 * j + c + 1 + 4 * i)
                    dve.wait_ge(b["raw"], 2 * j + c + 1 + 4 * i)
                    if j == 0 and isinstance(i, int) and c == 0:
                        dve.wait_ge(b["gq8"], 1)
                    if not (isinstance(i, int) and j < 2):
                        dve.wait_ge(b["z"], 8 * (j - 1) + 16 * i)
                    dve.scalar_tensor_tensor(sb_qk[:, par_, c, :], sb_raw[:, c, :], gain, sb_r[:, c, :],
                                             ALU.mult, ALU.mult).then_inc(b["qk"], 1)
                if not (isinstance(i, int) and j < 2):
                    dve.wait_ge(b["pv"], 8 * (j - 1) + 16 * i)
                if isinstance(i, int):
                    src = v_tok[:, :, j * P:j * P + P]
                else:
                    src = v_tok[:, :, bass.ds(2 * P * i + j * P, P)]
                dve.tensor_copy(sb_v[:, par_, :, :], src).then_inc(b["v"], 1)

            def softplus(u, j, i):
                n = 8 * j + u
                kb = 3 - u % 4
                w = T - P * kb
                off = (0, 128, 384, 768)[u % 4]
                dve.wait_ge(b["ln1"], n + 1 + 16 * i)
                if not (isinstance(i, int) and n < 8):
                    dve.wait_ge(b["cum"], 8 * j + 4 * (u // 4) - 4 + 16 * i)
                dve.scalar_tensor_tensor(sb_sp[:, u // 4, off:off + w], ps[2 + u % 4][:, 0:w], 0.0,
                                         sb_t[:, u % 2, 0:w], ALU.max, ALU.add).then_inc(b["sp"], 1)
                if kb < 3:
                    m = 6 * j + 3 * (u // 4) + u % 4 - 1
                    own, to = sb_sp[:, u // 4, off:off + w], slice(off - P, off - P + w)
                    dve.wait_ge(b["sp"], n + 1 + 16 * i)
                    dve.tensor_copy(sp_hi[:, u // 4, to], own).then_inc(b["sph"], 1)
                    dve.wait_ge(b["sph"], m + 1 + 12 * i)
                    dve.tensor_tensor(sp_lo[:, u // 4, to], own, sp_hi[:, u // 4, to].bitcast(F32), ALU.subtract)\
                        .then_inc(b["spl"], 1)

            dve.wait_ge(proj_free, 2 * (t0 + 4))
            raws(t0 + 4, 0)
            scaled(0)

            def evac(j, i):
                dve.wait_ge(b["pv"], 8 * j + 8 + 16 * i)
                dst = o_sb[:, j, :] if isinstance(i, int) else o_sb[:, j + 2 * i, :]
                dve.tensor_copy(dst, ps[6 + j % 2][:, :]).then_inc(b["ev"], 1)

            def pair(j, i, first, last):
                t = t0 + 4 + j
                for u in range(8):
                    softplus(u, j, i)
                    if u == 3 and not last:
                        raws(t + 1, j + 1, i)
                    if u == 4 and not first:
                        evac(j - 1, i)
                    if u == 5 and not last:
                        scaled(j + 1, i)

            pair(0, 0, True, False)
            with dve.Fori(0, 3) as i:
                pair(1, i, False, False)
                pair(2, i, False, False)
            pair(7, 0, False, True)
            evac(7, 0)

            def gate_step(t, i, k):
                for c in range(2):
                    n = 2 * k + c
                    slot = 2 * (k % 2) + c
                    dve.wait_ge(b["gate"], n + 1 + 4 * i)
                    if not (isinstance(i, int) and k < 2):
                        dve.wait_ge(y_done, y_base[l] + n - 3 + 4 * i)
                    if isinstance(i, int) and k == 0:
                        dve.wait_ge(b["ev"], 8)
                    dve.tensor_tensor(yf[:, slot, :], o_sb[:, n + 4 * i, :], gate[:, slot, :], ALU.mult).then_inc(yf_done, 1)
                    dve.sem_inc(proj_free, 1)
                if not (isinstance(i, int) and k == 0):
                    y_lows2(l, k - 1, i)

            walk(dve, t0 + 12, 4, gate_step)
            y_lows2(l, 3)
            out_steps(l, t0 + 16, 4, 2)

        def shortconv(l):
            t0, cw = tile_base[l], cols[l]["conv"]
            dve.memset(sc_cu[:, 0:2], 0.0).then_inc(c_["zero"], 1)
            dve.wait_ge(c_["zero"], 1)

            def low(k, i=0):
                dve.wait_ge(yhi_done, y_base[l] + k + 1 + i)
                src = y_hi[:, y_at(k), :] if isinstance(i, int) else y_hi[:, (k + 8) % 16 + i, :]
                dve.tensor_tensor(y_lo[:, k + i, :], sc_yf[:, :], src.bitcast(F32), ALU.subtract).then_inc(y_done, 1)

            def group(j, i, first=False):
                t = t0 + 2 * j
                if not first:
                    times_u(t, i, j)
                    dve.wait_ge(c_["y"], j + i)

                def w(m):
                    if isinstance(i, int):
                        return par[:, cw + 3 * j + m:cw + 3 * j + m + 1]
                    return par[:, bass.ds(3 * i + (cw + 3 * j + m), 1)]

                n = 2 * j + 2 * i
                dve.tensor_scalar(sc_acc[:, :], sc_cu[:, 2:T + 2], w(2), None, ALU.mult).then_inc(c_["cstep"], 1)
                dve.wait_ge(c_["cstep"], n + 1)
                dve.scalar_tensor_tensor(sc_acc[:, :], sc_cu[:, 1:T + 1], w(1), sc_acc[:, :], ALU.mult, ALU.add)\
                    .then_inc(c_["cstep"], 1)
                dve.wait_ge(c_["cstep"], n + 2)
                dve.scalar_tensor_tensor(sc_acc[:, :], sc_cu[:, 0:T], w(0), sc_acc[:, :], ALU.mult, ALU.add)\
                    .then_inc(c_["conv"], 1)
                if not first:
                    low(j - 1, i)
                dve.wait_ge(c_["conv"], j + 1 + i)
                dve.wait_ge(proj_done, 2 * t + 3 + 4 * i)
                if not first:
                    dve.wait_ge(yf_done, y_base[l] + j + i)
                dve.tensor_tensor(sc_y[:, :], bank(t + 1, 0)[:, :], sc_acc[:, :], ALU.mult).then_inc(c_["y"], 1)
                dve.wait_ge(c_["y"], j + 1 + i)
                dve.wait_ge(c_["gate"], j + 1 + i)
                dve.sem_inc(proj_free, 2)
                if not first:
                    dve.wait_ge(y_done, y_base[l] + j + i)
                dve.tensor_tensor(sc_yf[:, :], sc_y[:, :], sc_gate[:, :], ALU.mult).then_inc(yf_done, 1)

            group(0, 0, True)
            with dve.Fori(0, 8) as i:
                group(1, i)
            with dve.Fori(0, 7) as i:
                group(9, i)
            low(15)
            out_steps(l, t0 + 32, 8, 1)

        dve.wait_ge(par_loaded, 16)
        for m in range(KD):
            dve.wait_ge(x_loaded[m // 2], 16)
            gain_x(0, m)
            if m:
                low_x(0, m - 1)
                sum_squares(0, m - 1)
        low_x(0, KD - 1)
        for l, kind in enumerate(layers):
            norm(l)
            (deltanet, stickbreak, shortconv)[kind](l)

    @blk.tensor
    def _(pe):
        def passes(out_, w_h, w_l, m_h, m_l, start, stop):
            pe.matmul(out_, w_h, m_h, start=start, stop=False)
            pe.matmul(out_, w_h, m_l, start=False, stop=False)
            return pe.matmul(out_, w_l, m_h, start=False, stop=stop)

        def ready(t, i=0):
            pe.wait_ge(lo_done, t + 1 + 2 * i)
            if not (isinstance(i, int) and t < 2):
                pe.wait_ge(proj_free, 2 * (t - 1) + 4 * i)

        def in_block(t, c, k, bk=None):
            bk = bank(t, c) if bk is None else bk
            w = slice(k * 2 * P + c * P, k * 2 * P + c * P + P)
            return passes(bk[:, :], w_hi[:, t % 2, w], w_lo[:, t % 2, w], h_hi[:, k, :], h_lo[:, k, :],
                          k == 0, k == KD - 1)

        def in_tile(t, i=0):
            ready(t, i)
            for c in range(2):
                for k in range(KD):
                    mm = in_block(t, c, k)
                mm.then_inc(proj_done, 1)

        def sum_x(l):
            if l == 0:
                pe.wait_ge(loaded, 32)
            pe.wait_ge(sum_done, (KD - 1) * (l + 1))
            pe.matmul(ps[7][:, :], ones, rstd[:, :], start=True, stop=False)
            pe.wait_ge(sq_done, KD * (l + 1))
            pe.matmul(ps[7][:, :], ones, sq[:, (KD - 1) % 2, :], start=False, stop=True).then_inc(ss_done, 1)

        def in_part(t, c, k, start, stop):
            return in_block(t, c, k)

        def first_tiles(l, part, parts0, parts1, midway=None):
            t0 = tile_base[l]
            ready(t0)
            for k in range(KD):
                pe.wait_ge(h_done, 2 * KD * l + k + 1)
                for u, n in parts0:
                    mm = part(t0, u, k, k == 0, k == KD - 1)
                    if k == KD - 1 and n:
                        mm.then_inc(first_done, n)
                if k == (3 if l else KD - 2):
                    sum_x(l)
            ready(t0 + 1)
            for k in range(KD):
                for u, n in parts1:
                    mm = part(t0 + 1, u, k, k == 0, k == KD - 1)
                    if k == KD - 1 and n:
                        mm.then_inc(first_done, n)
                if k < KD - 1:
                    mm.then_inc(first_used, 1)
                if k == 4 and midway:
                    midway()

        def third_tile(l, part, parts):
            t = tile_base[l] + 2
            ready(t)
            for k in range(KD):
                pe.wait_ge(h_done, 2 * KD * l + KD + k + 1)
                if k == KD - 1:
                    pe.wait_ge(proj_done, 2 * t)
                    if layers[l] == SB:
                        pe.wait_ge(proj_free, 2 * t)
                for u, n in parts:
                    mm = part(t, u, k, k == 0, k == KD - 1)
                    if k == KD - 1 and n:
                        mm.then_inc(proj_done, n)

        def out_steps(l, first, n, per):
            def step(t, i, k):
                ready(t, i)
                first_step = isinstance(i, int) and k == 0
                for c in range(per):
                    kn_ = 16 // per
                    for kk in range(kn_):
                        if first_step and c == 0:
                            pe.wait_ge(y_done, y_base[l] + kk + 1)
                        w = slice(kk * per * P + c * P, kk * per * P + c * P + P)
                        mm = passes(bank(t, c)[:, :], w_hi[:, t % 2, w], w_lo[:, t % 2, w],
                                    y_hi[:, y_at(kk), :], y_lo[:, kk, :], kk == 0, kk == kn_ - 1)
                    mm.then_inc(proj_done, 2 // per)
            walk(pe, first, n, step)

        def deltanet(l):
            d, t0 = nth[l], tile_base[l]
            first_tiles(l, in_part, [(0, 2)], [(0, 1), (1, 1)])
            third_tile(l, in_part, [(0, 1), (1, 1)])
            with pe.Fori(0, 3) as i:
                in_tile(t0 + 3, i)
                in_tile(t0 + 4, i)

            for k in range(HEADS // 2):
                in_tile(t0 + 9 + k)
                for h in (2 * k, 2 * k + 1):
                    pe.wait_ge(ksq_done, HEADS * d + h + 1)
                    sel = cf[:, C_SELK + 8 * h:C_SELK + 8 * h + 8]
                    pe.matmul(ps[7][0:8, :], sel, ksq[:, h % 2, :], start=(h == 0), stop=(h == HEADS - 1))\
                        .then_inc(kss_done, 1)
            for k in range(4):
                in_tile(t0 + 13 + k)

            def spread(q, bk, g, block_):
                for h in range(GR):
                    hh = GR * g + h
                    mm = pe.matmul(bk[:, h * P:h * P + P], cb[0:96, B_SEL + hh * P:B_SEL + hh * P + P],
                                   row_parts[0:96, q, block_], start=(h == 0), stop=(h == GR - 1),
                                   skip_group_check=True)
                return mm

            def convolved(n):
                last = t0 + 16
                return 2 * last + (n % 2 + 1 if n // 2 == last % 2 else 0)

            with pe.Fori(0, NB) as bi:
                def v(per, k):
                    return NB * d * per + bi * per + k

                n_l = LEVELS - 1
                now = bass.ts(bi, P)
                pe.wait_ge(parts_done, 3 * d + 3)
                for g in range(NG):
                    pe.wait_ge(s["vne"], v(4, 1))
                    spread(1, ps[4 + g], g, now).then_inc(s["bbc"], 1)
                for g in range(NG):
                    pe.wait_ge(s["wneg"], v(2, 1))
                    pe.wait_ge(proj_free, convolved(2 + g))
                    spread(2, ps[2 + g], g, now).then_inc(s["rkbc"], 1)
                for g in range(NG):
                    pe.wait_ge(s["sst"], NB * d * 8 + 8 * d + 8 + bi * 8)
                    pe.wait_ge(proj_free, convolved(g))
                    spread(0, ps[g], g, now)
                    pe.matmul(ps[g][:, :], cb[:, B_ID:B_ID + P],
                              cb[:, B_INCL:B_INCL + P].unsqueeze(1).to_broadcast([P, GR, P]),
                              start=False, stop=True, skip_group_check=True).then_inc(s["gmask"], 1)
                pe.wait_ge(s["rows_b"], v(1, 1))
                pe.wait_ge(s["oe"], v(4, 1))
                pe.transpose(ps[6][:, 0:P], rows_b[:, :], ident).then_inc(s["tokt"], 1)

                def v_turn(p):
                    bk = ps[(7, 6, 2, 3)[p]]
                    src = prod if p < 2 else l_t
                    pe.wait_ge(s["vstage"] if p < 2 else s["vstage2"], v(1, 1))
                    for c in range(4):
                        mm = pe.transpose(bk[:, c * P:c * P + P], src[:, 4 * (p % 2) + c, :], ident)
                    mm.then_inc(s["vt"], 1)

                v_turn(0)
                pe.wait_ge(s["tok"], v(1, 1))
                v_turn(1)
                for g in range(NG):
                    pe.wait_ge(s["kbeta"], v(2, g + 1))
                    for h in range(GR):
                        mm = pe.matmul(ps[4 + g][:, h * P:h * P + P], kn[:, GR * g + h, :], k_beta[:, GR * g + h, :],
                                       start=True, stop=True)
                    mm.then_inc(s["kk"], 1)
                v_turn(2)
                v_turn(3)
                for g in range(NG):
                    pe.wait_ge(s["vb"], v(4, g + 1))
                    for h in range(GR):
                        mm = pe.matmul(ps[7 - g][:, h * P:h * P + P], kn[:, GR * g + h, :],
                                       big[:, GR * g + h, bass.ts(bi, P)], start=True, stop=True)
                    mm.then_inc(s["qk"], 1)
                for g in range(NG):
                    pe.wait_ge(s["u0i"], v(2, g + 1))
                    pe.wait_ge(s["dec"], v(8, GR * g + GR))
                    for h in range(GR):
                        mm = pe.transpose(ps[g][:, h * P:h * P + P], inv_t[:, GR * g + h, :], ident)
                    mm.then_inc(s["xt"], 1)
                    pe.wait_ge(s["lt"], v(2, g + 1))
                    spread(0, ps[4 + g], g, now).then_inc(s["gbc2"], 1)
                for lv in range(n_l):
                    for g in range(NG):
                        if lv == 0:
                            pe.wait_ge(s["x0"], v(2, g + 1))
                            pe.wait_ge(s["vb"], v(4, 3 + g))
                        else:
                            pe.wait_ge(s["xe"], v(2 * (n_l - 1), 2 * lv + g - 1))
                        for h in range(GR):
                            mm = pe.matmul(ps[2 + g][:, h * P:h * P + P], l_t[:, GR * g + h, :], inv[:, GR * g + h, :],
                                           start=True, stop=True)
                        mm.then_inc(s["pm"], 1)
                    if lv == 0:
                        for g in range(NG):
                            pe.wait_ge(s["x0"], v(2, g + 1))
                            for h in range(GR):
                                mm = pe.transpose(ps[g][:, h * P:h * P + P], kn[:, GR * g + h, :], ident)
                            mm.then_inc(s["ktok"], 1)
                    for g in range(NG):
                        pe.wait_ge(s["pe_p"], v(2 * n_l, 2 * lv + g + 1))
                        if lv:
                            pe.wait_ge(s["ue"], v(2 * n_l, 2 * lv + g - 1))
                        else:
                            pe.wait_ge(s["eg"], v(2, g + 1))
                        for h in range(GR):
                            mm = pe.matmul(ps[4 + g][:, h * P:h * P + P], prod[:, GR * g + h, :], inv_t[:, GR * g + h, :],
                                           start=True, stop=True)
                        mm.then_inc(s["du"], 1)
                    if lv < n_l - 1:
                        for g in range(NG):
                            pe.wait_ge(s["ue"], v(2 * n_l, 2 * lv + g + 1))
                            if lv == 0:
                                pe.wait_ge(s["at"], v(2, 2 - g))
                            for h in range(GR):
                                mm = pe.transpose(ps[6 + g][:, h * P:h * P + P], inv_t[:, GR * g + h, :], ident)
                            mm.then_inc(s["turned"], 1)
                def state_out(p):
                    if p >= 2:
                        pe.wait_ge(s["oe"], v(4, p))
                    for e in range(2):
                        h = 2 * p + e
                        for c in range(2):
                            o_ = ps[6 + p % 2][:, (2 * e + c) * P:(2 * e + c + 1) * P]
                            mm = pe.matmul(o_, state[:, h, c * P:c * P + P], q_dec[:, h, :], start=(e == 0 and c == 0),
                                           stop=False, skip_group_check=True)
                    mm.then_inc(s["ot0"], 1)

                pe.wait_ge(s["qdec"], v(2, 2))
                pe.wait_ge(s["xe"], v(2 * (n_l - 1), 2 * (n_l - 1)))
                state_out(0)
                state_out(1)
                for g in range(NG):
                    pe.wait_ge(s["kin"], v(2, g + 1))
                    pe.wait_ge(s["ue"], v(2 * n_l, 2 * n_l - 1 + g))
                    for h in range(GR):
                        mm = pe.matmul(ps[2 + g][:, h * P:h * P + P], k_in[:, GR * g + h, :], inv_t[:, GR * g + h, :],
                                       start=True, stop=True)
                    mm.then_inc(s["wt"], 1)

                def v_new(p):
                    if p < 2:
                        pe.wait_ge(s["wneg"], v(2, p // 2 + 2))
                        pe.wait_ge(s["ue"], v(2 * n_l, 2 * n_l))
                    else:
                        pe.wait_ge(s["wneg"], v(2, 3))
                        pe.wait_ge(s["vne"], v(4, p))
                    for e in range(2):
                        h = 2 * p + e
                        o_ = ps[4 + p % 2][:, e * 2 * P:(e + 1) * 2 * P]
                        pe.matmul(o_, inv_t[:, h, :], vb[:, h, :], start=True, stop=False)
                        mm = pe.matmul(o_, w_neg[:, h, :], state[:, h, :], start=False, stop=True)
                    mm.then_inc(s["vn"], 1)

                def o_t(p):
                    pe.wait_ge(s["vne"], v(4, p + 2))
                    pe.wait_ge(s["kout"], v(2, 2))
                    if p >= 2:
                        pe.wait_ge(s["sst"], NB * d * 8 + 8 * d + 8 + bi * 8 + 2 * (p - 1))
                    for e in range(2):
                        h = 2 * p + e
                        mm = pe.matmul(ps[p % 2][:, e * 2 * P:(e + 1) * 2 * P], k_out[:, h, :], vb[:, h, :],
                                       start=True, stop=True)
                    mm.then_inc(s["su"], 1)
                    for e in range(2):
                        h = 2 * p + e
                        for c in range(2):
                            o_ = ps[6 + p % 2][:, (2 * e + c) * P:(2 * e + c + 1) * P]
                            mm = pe.matmul(o_, vb[:, h, c * P:c * P + P], attn_t[:, h, :], start=False, stop=True,
                                           skip_group_check=True)
                    mm.then_inc(s["ot"], 1)

                v_new(0)
                for p in range(4):
                    if p < 3:
                        v_new(p + 1)
                    if p >= 2:
                        state_out(p)
                    o_t(p)

            for h in range(HEADS):
                n = HEADS * d + h
                pe.wait_ge(nsum_done, 2 * n + 2)
                if h:
                    pe.wait_ge(nln_done, n)
                pe.matmul(ps[4][:, :], ones, nsq[:, 0, :], start=True, stop=True).then_inc(nss_done, 1)
                in_tile(dn_gate0[l] + h)
            out_steps(l, dn_gate0[l] + 8, 8, 1)

        def stickbreak(l):
            t0 = tile_base[l]

            def v_part(t, tb, k_, start):
                o_ = bank(t, tb // 2)[:, (tb % 2) * 2 * P:(tb % 2 + 1) * 2 * P]
                tk = slice(tb * P, tb * P + P)
                w = slice(k_ * 2 * P, (k_ + 1) * 2 * P)
                hh, hl, wh, wl = h_hi[:, k_, tk], h_lo[:, k_, tk], w_hi[:, t % 2, w], w_lo[:, t % 2, w]
                last = k_ == KD - 1
                pe.matmul(o_, hh, wh, start=start, stop=False, skip_group_check=True)
                pe.matmul(o_, hh, wl, start=False, stop=False, skip_group_check=True)
                return pe.matmul(o_, hl, wh, start=False, stop=last, skip_group_check=True)

            def turn_rstd():
                pe.wait_ge(rstd_done, l + 1)
                for tb in range(NB):
                    mm = pe.matmul(ps[6][:, tb:tb + 1], rstd[:, tb * P:tb * P + P], cf[:, C_ID:C_ID + 1],
                                   start=True, stop=True)
                mm.then_inc(turned_rstd, 1)

            tb_parts = [(tb, tb % 2) for tb in range(NB)]

            def side_by_side(t, tb, k, start, stop):
                return v_part(t, tb, k, start and tb % 2 == 0)

            first_tiles(l, side_by_side, tb_parts, tb_parts, turn_rstd)
            third_tile(l, side_by_side, tb_parts)
            ready(t0 + 3)
            for tb in range(NB):
                for k_ in range(KD):
                    mm = v_part(t0 + 3, tb, k_, k_ == 0)
                if tb % 2:
                    mm.then_inc(proj_done, 1)

            def qk_ready(t, i):
                pe.wait_ge(lo_done, t + 1 + 2 * i)
                pe.wait_ge(proj_free, 2 * t + 4 * i)

            def qk_part(t, i, c, k):
                mm = in_block(t, c, k, bk=ps[c])
                if k == KD - 1:
                    mm.then_inc(proj_done, 1)

            def sums(j, i=0):
                for c in range(2):
                    pe.wait_ge(b["sq"], 2 * j + c + 1 + 4 * i)
                    pe.wait_ge(b["raw"], 2 * j + c + 1 + 4 * i)
                    pe.matmul(ps[c][:, :], cf[:, C_BLOCK:C_BLOCK + P], sb_sq[:, c, :], start=True, stop=True)\
                        .then_inc(b["ss"], 1)

            qk_ready(t0 + 4, 0)
            for c in range(2):
                for k in range(KD):
                    qk_part(t0 + 4, 0, c, k)
            sums(0)

            def geometry(u):
                kb = 3 - u % 4
                return kb, T - P * kb, u // 4

            def z(u, j, i):
                n = 8 * j + u
                kb, w, e = geometry(u)
                qs = slice(kb * P, T)
                rr = slice(64 * e, 64 * e + 64)
                bk = ps[2 + u % 4]
                if u == 0:
                    pe.wait_ge(b["qk"], 2 * j + 2 + 4 * i)
                    pe.wait_ge(b["v"], j + 1 + 2 * i)
                if not (isinstance(i, int) and n < 4):
                    pe.wait_ge(b["w"], n - 3 + 16 * i)
                pe.matmul(bk[:, 0:w], sb_qk[rr, j % 2, 1, kb * P:kb * P + P], sb_qk[rr, j % 2, 0, qs],
                          start=True, stop=False, skip_group_check=True)
                pe.matmul(bk[:, 0:P], cb[:, B_ID:B_ID + P], cb[:, B_STRICT:B_STRICT + P],
                          start=False, stop=True, skip_group_check=True).then_inc(b["z"], 1)

            def cum(n, i):
                u = n % 8
                kb, w, e = geometry(u)
                bk = ps[2 + u % 4]
                if kb == 3:
                    pe.wait_ge(b["sp"], n + 1 + 16 * i)
                else:
                    if isinstance(i, int) and n == 1:
                        pe.wait_ge(b["tri"], 1)
                    pe.wait_ge(b["spl"], 6 * (n // 8) + 3 * e + u % 4 + 12 * i)
                for kb2 in range(kb, NB):
                    w2 = T - P * kb2
                    off = (0, 128, 384, 768)[3 - kb2]
                    c = 0 if kb2 == kb else P
                    if kb2 == 3:
                        mm = pe.matmul(bk[:, w - w2:w], cf[:, C_TRI + c:C_TRI + c + P], sb_sp[:, e, 0:w2], start=False, stop=True,
                                       skip_group_check=True)
                        continue
                    for part in (sp_hi, sp_lo):
                        pe.matmul(bk[:, w - w2:w], tri_r[:, c:c + P], part[:, e, off - P:off - P + w2],
                                  start=False, stop=False, skip_group_check=True)
                mm.then_inc(b["cum"], 1)

            def pv(n, i):
                u = n % 8
                j = n // 8
                kb, w, e = geometry(u)
                pe.wait_ge(b["w"], n + 1 + 16 * i)
                if u % 8 == 0 and not (isinstance(i, int) and j < 2):
                    pe.wait_ge(b["ev"], j + 2 * i)
                pe.matmul(ps[6 + j % 2][64 * e:64 * e + 64, kb * P:T], sb_v[:, j % 2, kb, 64 * e:64 * e + 64],
                          sb_w[:, u % 2, 0:w], start=(kb == 3), stop=(kb == 0), skip_group_check=True)\
                    .then_inc(b["pv"], 1)

            parts = [(c, k) for c in range(2) for k in range(KD)]
            share = [4, 4, 4, 4]

            def pair(j, i, first, last):
                t = t0 + 4 + j
                rest = list(parts)
                for u in range(8):
                    z(u, j, i)
                    if not last:
                        if u == 0:
                            qk_ready(t + 1, i)
                        if u < len(share):
                            for _ in range(share[u]):
                                qk_part(t + 1, i, *rest.pop(0))
                    if not (first and u < 2):
                        cum(8 * j + u - 2, i)
                    if not (first and u < 3):
                        pv(8 * j + u - 3, i)
                    if u == 5 and not last:
                        sums(j + 1, i)

            pair(0, 0, True, False)
            with pe.Fori(0, 3) as i:
                pair(1, i, False, False)
                pair(2, i, False, False)
            pair(7, 0, False, True)
            cum(62, 0)
            pv(61, 0)
            cum(63, 0)
            pv(62, 0)
            pv(63, 0)
            def gate_step(t, i, k):
                if isinstance(i, int) and k == 0:
                    pe.wait_ge(proj_free, 2 * t)
                in_tile(t, i)
            walk(pe, t0 + 12, 4, gate_step)
            out_steps(l, t0 + 16, 4, 2)

        def shortconv(l):
            t0 = tile_base[l]
            first_tiles(l, in_part, [(0, 1), (1, 1)], [(0, 1), (1, 1)])
            third_tile(l, in_part, [(0, 1), (1, 1)])
            in_tile(t0 + 3)
            with pe.Fori(0, 14) as i:
                in_tile(t0 + 4, i)
                in_tile(t0 + 5, i)
            out_steps(l, t0 + 32, 8, 1)

        for n in PE_AHEAD:
            pe.sem_inc(s[n], 1)
        for l, kind in enumerate(layers):
            (deltanet, stickbreak, shortconv)[kind](l)

    block.__exit__(None, None, None)


def constants():
    import numpy as np
    i, j = np.arange(P)[:, None], np.arange(P)[None, :]
    f = np.zeros((P, NCF), np.float32)
    f[:, C_ID:C_ID + P] = i == j
    f[:, C_ONES:C_ONES + P] = 1
    f[:, C_BLOCK:C_BLOCK + P] = i // 64 == j // 64
    f[:, C_TRI:C_TRI + P] = -1.0 * (i >= j)
    f[:, C_NEG:C_NEG + P] = -1
    for h in range(HEADS):
        f[:, C_SELK + 8 * h + h] = 1
    g = np.zeros((P, NCB), np.float32)
    g[:, B_ID:B_ID + P] = i == j
    g[:, B_SUB:B_SUB + P] = -1.0 * ((i % 2 == 0) & (j == i + 1))
    g[:, B_STRICT:B_STRICT + P] = -1e30 * (i >= j)
    g[:, B_INCL:B_INCL + P] = -1e30 * (i > j)
    for lv in range(LEVELS - 1):
        w = 2 << lv
        g[:, B_LEVEL + lv * P:B_LEVEL + lv * P + P] = (i // w % 2 == 1) & (j // w == i // w - 1)
    for h in range(HEADS):
        g[:, B_SEL + h * P:B_SEL + h * P + P] = (i % 32 == h) & (i < 3 * 32)
    return f, g.astype(mybir.dt.np(BF16))


def by_tiles(w, chunks):
    import numpy as np
    k = w.shape[0] // P
    w = w.reshape(k, P, w.shape[1])
    return [np.ascontiguousarray(w[:, :, c].transpose(1, 0, 2)).reshape(P, WT) for c in chunks]


def lay_out(layers, inp):
    import numpy as np
    cols, n = param_columns(layers)
    par = np.zeros((P, n), np.float32)
    tiles = []
    seen = {DN: 0, SB: 0, SC: 0}
    ar = np.arange
    for l, kind in enumerate(layers):
        c, j = cols[l], seen[kind]
        seen[kind] += 1
        par[:, c["norm"]:c["norm"] + KD] = inp["norm_g"][l].reshape(KD, P).T
        if kind == DN:
            w, wo = inp["dn_w_in"][j], inp["dn_w_out"][j]
            ab = np.zeros((D, 2 * P), np.float32)
            ab[:, 0:8], ab[:, 32:40] = w[:, 6144:6152], w[:, 6152:6160]
            tiles += by_tiles(ab, [ar(2 * P)])
            tiles += by_tiles(w, [ar(m * 2 * P, (m + 1) * 2 * P) for m in range(24)])
            tiles += by_tiles(wo, [ar(m * P, (m + 1) * P) for m in range(8)])
            cw = inp["dn_conv_w"][j]
            par[:, c["conv"]:c["conv"] + 128] = cw.reshape(4, 32, P).transpose(2, 1, 0).reshape(P, 128)
            par[0:8, c["dt"]] = inp["dn_dt_bias"][j]
            par[0:8, c["alog"]] = inp["dn_a_log"][j]
            par[:, c["onorm"]:c["onorm"] + 2] = inp["dn_o_norm_g"][j].reshape(2, P).T
        elif kind == SB:
            w, wo = inp["sb_w_in"][j], inp["sb_w_out"][j]
            tiles += by_tiles(w, [2 * D + ar(m * 2 * P, (m + 1) * 2 * P) for m in range(4)])
            tiles += by_tiles(w, [np.concatenate([ar(m * P, (m + 1) * P), D + ar(m * P, (m + 1) * P)]) for m in range(8)])
            tiles += by_tiles(w, [3 * D + ar(m * 2 * P, (m + 1) * 2 * P) for m in range(4)])
            tiles += by_tiles(wo, [ar(m * 2 * P, (m + 1) * 2 * P) for m in range(4)])
            par[:, c["q"]] = np.tile(inp["sb_q_norm_g"][j], 2)
            par[:, c["k"]] = np.tile(inp["sb_k_norm_g"][j], 2)
        else:
            w, wo = inp["sc_w_in"][j], inp["sc_w_out"][j]
            for m in range(16):
                ch = [q * 2 * D + ar(m * P, (m + 1) * P) for q in range(4)]
                tiles += by_tiles(w, [np.concatenate([ch[1], ch[2]]), np.concatenate([ch[0], ch[3]])])
            tiles += by_tiles(wo, [ar(m * P, (m + 1) * P) for m in range(8)])
            par[:, c["conv"]:c["conv"] + 48] = inp["sc_conv_w"][j].reshape(3, 16, P).transpose(2, 1, 0).reshape(P, 48)
    return np.stack(tiles), par


def arrays_of(layers, inp):
    import numpy as np
    tiles, par = lay_out(layers, inp)
    f, g = constants()
    x = np.ascontiguousarray(inp["x"][0].T.reshape(KD, P, T).transpose(1, 0, 2))
    return {"x_t": x, "w_tiles": tiles, "params": par, "const_f": f, "const_b": g}


def build(nc, layers, arrays):
    import numpy as np
    args = [nc.dram_tensor(n, a.shape, mybir.dt.from_np(a.dtype), kind="ExternalInput").ap() for n, a in arrays.items()]
    out = nc.dram_tensor("out_t", (P, KD, T), F32, kind="ExternalOutput").ap()
    trunk(nc, layers, *args, out)


def kernel(**inputs):
    import numpy as np
    import concourse.bacc as bacc
    from concourse.bass_utils import run_bass_kernel_spmd as run

    layers = [DN, SB, SC, DN]
    inp = {k: np.asarray(v) for k, v in inputs.items()}
    arrays = arrays_of(layers, inp)
    nc = bacc.Bacc("TRN2", target_bir_lowering=False, num_devices=1, dynamic_dma_scratch_size=1024)
    build(nc, layers, arrays)
    r = run(nc, [arrays], core_ids=[0])
    got = r.results[0]["out_t"]
    return np.ascontiguousarray(got.transpose(1, 0, 2).reshape(D, T).T).reshape(1, T, D)
```
